# Optimizing a Trainium2 kernel written in Bass

```python
import math
import jax
import jax.numpy as jnp
from jax import lax
import numpy as np

D_MODEL = 2048
BATCH = 1
SEQ = 256
DEPTH = 2

HEAD_DIM = 64
N_HEADS_A = 12
DILATED_CONFIGS = ((128, 1), (512, 4), (2048, 16))
DILATED_BLOCK = 64
N_HEADS_B = 10
N_KV_B = 2
WINDOW_B = 128
BLOCK_B = 128
N_HEADS_C = 10
GRID_W = 64
NA_ROWS = 8
NA_COLS = 16
WIDTH_A = N_HEADS_A * HEAD_DIM
WIDTH_B = N_HEADS_B * HEAD_DIM
WIDTH_B_KV = N_KV_B * HEAD_DIM
WIDTH_C = N_HEADS_C * HEAD_DIM
MIX_WIDTH = WIDTH_A + WIDTH_B + WIDTH_C
IN_COLS = 3 * WIDTH_A + WIDTH_B + 2 * WIDTH_B_KV + 3 * WIDTH_C
D_FF = 5632
CONV_WIDTH = 3
ROPE_THETA = 10000.0
EPS = 1e-6
NEG_INF = -1e30

kernel_name = 'hybrid_parallel_local_attention_encoder'

def rms_normalize(x):
    x32 = x.astype(jnp.float32)
    return (x32 * lax.rsqrt(jnp.mean(x32 * x32, axis=-1, keepdims=True) + EPS)).astype(x.dtype)

def rmsnorm(x, gain):
    return rms_normalize(x) * gain

def heads(x, n):
    b, t, _ = x.shape
    return x.reshape(b, t, n, HEAD_DIM).transpose(0, 2, 1, 3)

def merge_heads(x):
    b, h, t, d = x.shape
    return x.transpose(0, 2, 1, 3).reshape(b, t, h * d)

def rotary(x):
    t, dh = x.shape[-2], x.shape[-1]
    inv_freq = ROPE_THETA ** (-jnp.arange(0, dh, 2, dtype=jnp.float32) / dh)
    ang = jnp.arange(t, dtype=jnp.float32)[:, None] * inv_freq[None, :]
    cos = jnp.cos(ang).astype(x.dtype)
    sin = jnp.sin(ang).astype(x.dtype)
    x1, x2 = x[..., : dh // 2], x[..., dh // 2:]
    return jnp.concatenate([x1 * cos - x2 * sin, x2 * cos + x1 * sin], axis=-1)

def banded_attention(q, k, v, half, block):
    n, g, length, dh = q.shape
    nb = length // block
    span = block + 2 * half
    kp = jnp.pad(k, ((0, 0), (half, half), (0, 0)))
    vp = jnp.pad(v, ((0, 0), (half, half), (0, 0)))
    idx = jnp.arange(nb)[:, None] * block + jnp.arange(span)[None, :]
    kb = kp[:, idx]
    vb = vp[:, idx]
    qb = q.reshape(n, g, nb, block, dh)
    s = jnp.einsum('ngbqd,nbkd->ngbqk', qb, kb).astype(jnp.float32) * (dh ** -0.5)
    qpos = jnp.arange(nb)[:, None] * block + jnp.arange(block)[None, :]
    kpos = idx - half
    valid = ((jnp.abs(qpos[:, :, None] - kpos[:, None, :]) <= half)
             & (kpos >= 0)[:, None, :] & (kpos < length)[:, None, :])
    s = jnp.where(valid, s, NEG_INF)
    lse = jax.nn.logsumexp(s, axis=-1)
    p = jnp.exp(s - lse[..., None]).astype(v.dtype)
    o = jnp.einsum('ngbqk,nbkd->ngbqd', p, vb)
    return o.reshape(n, g, length, dh), lse.reshape(n, g, length)

def to_strided(x, r):
    b, h, t, d = x.shape
    return x.reshape(b, h, t // r, r, d).transpose(0, 1, 3, 2, 4).reshape(b * h * r, t // r, d)

def from_strided(x, b, h, r):
    length = x.shape[1]
    rest = x.shape[2:]
    y = x.reshape((b, h, r, length) + rest)
    y = jnp.moveaxis(y, 2, 3)
    return y.reshape((b, h, length * r) + rest)

def dilated_attention(q, k, v):
    b, h, t, dh = q.shape
    outs, lses = [], []
    for window, r in DILATED_CONFIGS:
        length = t // r
        half = window // (2 * r)
        block = math.gcd(length, DILATED_BLOCK)
        o, lse = banded_attention(to_strided(q, r)[:, None], to_strided(k, r), to_strided(v, r), half, block)
        outs.append(from_strided(o[:, 0], b, h, r))
        lses.append(from_strided(lse[:, 0], b, h, r))
    weights = jax.nn.softmax(jnp.stack(lses), axis=0)
    return jnp.einsum('cbht,cbhtd->bhtd', weights.astype(q.dtype), jnp.stack(outs))

def sink_window_attention(q, k, v, sink):
    b, hq, t, dh = q.shape
    g = hq // N_KV_B
    o, lse = banded_attention(q.reshape(b * N_KV_B, g, t, dh), k.reshape(b * N_KV_B, t, dh),
                              v.reshape(b * N_KV_B, t, dh), WINDOW_B, BLOCK_B)
    sink_g = jnp.tile(sink.astype(jnp.float32).reshape(N_KV_B, g), (b, 1))[:, :, None]
    keep = jnp.exp(lse - jnp.logaddexp(lse, sink_g))
    return (o * keep[..., None].astype(o.dtype)).reshape(b, hq, t, dh)

def neighborhood_attention(q, k, v, rpb):
    b, h, t, dh = q.shape
    rows = t // GRID_W
    kr = min(NA_ROWS, rows)
    kc = NA_COLS
    r = jnp.arange(rows)
    c = jnp.arange(GRID_W)
    row_start = jnp.clip(r - kr // 2, 0, rows - kr)
    ridx = row_start[:, None] + jnp.arange(kr)[None, :]
    col_start = jnp.clip(c - kc // 2, 0, GRID_W - kc)
    col_mask = (c[None, :] >= col_start[:, None]) & (c[None, :] < col_start[:, None] + kc)
    qg = q.reshape(b, h, rows, GRID_W, dh)
    kg = k.reshape(b, h, rows, GRID_W, dh)[:, :, ridx]
    vg = v.reshape(b, h, rows, GRID_W, dh)[:, :, ridx]
    s = jnp.einsum('bhrcd,bhrkwd->bhrckw', qg, kg).astype(jnp.float32) * (dh ** -0.5)
    roff = (ridx - r[:, None]) + (NA_ROWS - 1)
    coff = jnp.clip(c[None, :] - c[:, None] + (kc - 1), 0, 2 * kc - 2)
    bias = rpb[:, roff[:, None, :, None], coff[None, :, None, :]]
    s = jnp.where(col_mask[:, None, :], s + bias.astype(jnp.float32)[None], NEG_INF)
    p = jax.nn.softmax(s.reshape(b, h, rows, GRID_W, kr * GRID_W), axis=-1)
    p = p.reshape(s.shape).astype(v.dtype)
    o = jnp.einsum('bhrckw,bhrkwd->bhrcd', p, vg)
    return o.reshape(b, h, t, dh)

def split_projection(proj):
    sizes = (WIDTH_A,) * 3 + (WIDTH_B, WIDTH_B_KV, WIDTH_B_KV) + (WIDTH_C,) * 3
    offsets = np.cumsum(sizes)[:-1].tolist()
    return jnp.split(proj, offsets, axis=-1)

def depthwise_conv(u, w, bias):
    t = u.shape[1]
    pad = CONV_WIDTH // 2
    up = jnp.pad(u, ((0, 0), (pad, pad), (0, 0)))
    return sum(up[:, j:j + t] * w[j] for j in range(CONV_WIDTH)) + bias

def setup_inputs(seed: int = 0) -> dict:
    key = jax.random.key(seed)
    ks = jax.random.split(key, 13)
    nrm = jax.random.normal
    f32 = jnp.float32
    return {
        'x': nrm(ks[0], (BATCH, SEQ, D_MODEL), f32),
        'ln_attn': 1.0 + 0.02 * nrm(ks[1], (DEPTH, D_MODEL), f32),
        'w_in': nrm(ks[2], (DEPTH, D_MODEL, IN_COLS), f32) * D_MODEL ** -0.5,
        'sink_b': 0.5 * nrm(ks[3], (DEPTH, N_HEADS_B), f32),
        'rpb_c': 0.1 * nrm(ks[4], (DEPTH, N_HEADS_C, 2 * NA_ROWS - 1, 2 * NA_COLS - 1), f32),
        'mix_gain': 1.0 + 0.02 * nrm(ks[5], (DEPTH, MIX_WIDTH), f32),
        'w_out': nrm(ks[6], (DEPTH, MIX_WIDTH, D_MODEL), f32) * MIX_WIDTH ** -0.5,
        'ln_ffn': 1.0 + 0.02 * nrm(ks[7], (DEPTH, D_MODEL), f32),
        'w_up': nrm(ks[8], (DEPTH, D_MODEL, 2 * D_FF), f32) * D_MODEL ** -0.5,
        'conv_w': nrm(ks[9], (DEPTH, CONV_WIDTH, 2 * D_FF), f32) * CONV_WIDTH ** -0.5,
        'conv_b': 0.01 * nrm(ks[10], (DEPTH, 2 * D_FF), f32),
        'w_down': nrm(ks[11], (DEPTH, D_FF, D_MODEL), f32) * D_FF ** -0.5,
        'ln_final': 1.0 + 0.02 * nrm(ks[12], (D_MODEL,), f32),
    }

def reference(x, ln_attn, w_in, sink_b, rpb_c, mix_gain, w_out, ln_ffn, w_up, conv_w, conv_b, w_down, ln_final):
    for l in range(DEPTH):
        h = rmsnorm(x, ln_attn[l])
        qa, ka, va, qb, kb, vb, qc, kc, vc = split_projection(h @ w_in[l])
        oa = dilated_attention(rotary(heads(qa, N_HEADS_A)), rotary(heads(ka, N_HEADS_A)), heads(va, N_HEADS_A))
        ob = sink_window_attention(rotary(heads(qb, N_HEADS_B)), rotary(heads(kb, N_KV_B)), heads(vb, N_KV_B), sink_b[l])
        oc = neighborhood_attention(heads(qc, N_HEADS_C), heads(kc, N_HEADS_C), heads(vc, N_HEADS_C), rpb_c[l])
        mixed = jnp.concatenate([rms_normalize(merge_heads(oa)), rms_normalize(merge_heads(ob)),
                                 rms_normalize(merge_heads(oc))], axis=-1) * mix_gain[l]
        x = x + mixed @ w_out[l]
        h = rmsnorm(x, ln_ffn[l])
        u = depthwise_conv(h @ w_up[l], conv_w[l], conv_b[l])
        gate, val = jnp.split(u, 2, axis=-1)
        x = x + (jax.nn.silu(gate) * val) @ w_down[l]
    return rmsnorm(x, ln_final)


_drawn_inputs = setup_inputs


def setup_inputs(seed=0):
    import zlib

    import numpy as np

    out = dict(_drawn_inputs(seed))
    spreads = {}
    factors = {'sink_b': 8.0, 'ln_ffn': 3.85, 'conv_b': 7.256, 'ln_final': 2.919}
    for name, (base, spread) in spreads.items():
        noise = np.random.default_rng([zlib.crc32(name.encode()), seed]).standard_normal(out[name].shape)
        drawn = base * np.exp(spread * noise) if base else spread * noise
        out[name] = jnp.asarray(drawn.astype(out[name].dtype))
    for name, factor in factors.items():
        out[name] = (out[name] * factor).astype(out[name].dtype)
    return out
```

```python
from contextlib import ExitStack

import numpy as np
import concourse.bass as bass
from concourse import mybir

P = 128
F32 = mybir.dt.float32
F32R = mybir.dt.float32r
ALU = mybir.AluOpType
ACT = mybir.ActivationFunctionType
AX = mybir.AxisListType

DEPTH, D, T, HD, D_FF = 2, 2048, 256, 64, 5632
HA, HB, HC, HKV = 12, 10, 10, 2
WA, WB, WKV, WC = HA * HD, HB * HD, HKV * HD, HC * HD
VCOLS = WA + WKV + WC
EPS = 1e-6
NEG = -1e30

KC = D // P
TT = T // P
NVB = VCOLS // 512
FC = D_FF // P
QUARTERS = 4
FQ = FC // QUARTERS

PA, PB, PC = HA // 2, HB // 2, HC // 2
PAIRS = PA + PB + PC
ROT = 2 * PA + 1 + PB
BRANCHES = ((0, WA), (WA, WB), (WA + WB, WC))

RING = 4
PIECE = 8 * P
PIECE_DOWN = FQ * P
G_V, G_PROJ, G_OUT, G_FFN = 0, 2 * NVB, 2 * NVB + 14, 2 * NVB + 14 + KC // 2
G_UP, G_DOWN = FQ, KC // 4
G_QUARTER = G_UP + G_DOWN
GROUPS = G_FFN + QUARTERS * G_QUARTER
MAIN = G_FFN

R_V, R_PROJ, R_MIX, R_OUT = 0, NVB, NVB + 14, NVB + 14 + KC // 2
R_FFN = R_OUT + KC // 2
R_QUARTER = FQ + KC // 2
ROUNDS = R_FFN + QUARTERS * R_QUARTER

O_LN1, O_MIX, O_LN2, O_CONV, O_SINK = 0, KC, 2 * KC, 3 * KC, 3 * KC + 8 * FC
NPAR = O_SINK + HB
O_COS, O_SIN, O_ROT, O_ID, O_ONE = 0, T, 2 * T, 2 * T + P, 2 * T + 2 * P
O_MASK = 2 * T + 3 * P
NCONST = O_MASK + 3 * TT * T

SEED_SLOT = RING
SEED_ACC = 1
SEED_SCORES = 1
SEED_HEAD = 2
SEED_PAIR = 1
SEED_ROT = 2
SEED_ROT_READ = 1
SEED_PROD = 1
SEED_SQ = 1


def build(nc, xT, w_main, w_up, w_down, bias_c, params, consts, outT):
    with ExitStack() as ctx:
        def sb(name, shape, dt=F32):
            return ctx.enter_context(nc.sbuf_tensor(name, shape, dt))

        def bank(name):
            return ctx.enter_context(nc.psum_tensor(name, [P, 512], F32))

        def sem(name):
            return ctx.enter_context(nc.semaphore(name))

        acc = [bank("acc0"), bank("acc1")]
        aux = bank("aux")
        scores_ps = [bank("scores0"), bank("scores1")]
        pt_ps = [bank("pt0"), bank("pt1")]
        o_ps = bank("o_ps")

        x = sb("x", [P, KC, T])
        h_hi, h_lo = sb("h_hi", [P, KC, T], F32R), sb("h_lo", [P, KC, T], F32R)
        mixed = sb("mixed", [P, TT, D])
        h_full = mixed.ap().rearrange("p t (k c) -> p (t k) c", c=T)
        v = sb("v", [P, TT, VCOLS])
        w_raw = sb("w_raw", [P, RING, PIECE_DOWN])
        w_hi = [sb(f"w_hi{s}", [P, PIECE_DOWN], F32R) for s in range(RING)]
        w_lo = [sb(f"w_lo{s}", [P, PIECE_DOWN], F32R) for s in range(RING)]
        with nc.sbuf_tensor("bias", [P, HC, TT * T], F32) as bias:
            pass
        act_hi, act_lo = sb("act_hi", [P, FQ, T], F32R), sb("act_lo", [P, FQ, T], F32R)
        par = sb("par", [P, DEPTH * NPAR + KC])
        con = sb("con", [P, NCONST])
        raw = [sb("raw0", [P, T]), sb("raw1", [P, T])]
        q_sb, k_sb = sb("q_sb", [P, T]), sb("k_sb", [P, T])
        rot_sin, rot_cos = sb("rot_sin", [P, T]), sb("rot_cos", [P, T])
        with nc.sbuf_tensor("s_sb", [P, 2, TT * T], F32) as s_sb:
            pass
        gate, value = sb("gate", [P, T]), sb("value", [P, T])
        silu, prod = sb("silu", [P, T]), sb("prod", [P, T])
        pt_sb = sb("pt_sb", [P, 2, TT * T])
        junk = sb("junk", [P, WA])
        mx, nmx = sb("mx", [P, 4]), sb("nmx", [P, 4])
        den, esink, den_all, rden = (sb(n, [P, 4]) for n in ("den", "esink", "den_all", "rden"))
        branch_ssq, branch_ms, branch_r = (sb(n, [P, 3, TT]) for n in ("branch_ssq", "branch_ms", "branch_r"))
        sq, sq_sum = sb("sq", [P, T]), sb("sq_sum", [P, T])
        ms, r_tok = sb("ms", [P, TT]), sb("r_tok", [P, TT])
        silu_first = sb("silu_first", [P, TT])
        minus_half, zeros = sb("minus_half", [P, TT]), sb("zeros", [P, T])
        diag = sb("diag", [P, TT, P])

        cos, sin = con[:, O_COS:O_COS + T], con[:, O_SIN:O_SIN + T]
        rot_m, ident, ones = (con[:, o:o + P] for o in (O_ROT, O_ID, O_ONE))
        mask_a, mask_b, mask_c = (con[:, O_MASK + b * TT * T:O_MASK + (b + 1) * TT * T] for b in range(3))

        landed = [sem(f"landed{s}") for s in range(RING)]
        x_landed, par_landed, id_landed, con_landed, mask_landed, bias_landed, stored = (
            sem(n) for n in ("x_landed", "par_landed", "id_landed", "con_landed", "mask_landed", "bias_landed",
                             "stored"))
        slot_used, v_tile0, rot_ready, scores_ready, transposed, pv_done, ssq_ready, r_ready, mixt_ready = (
            sem(n) for n in ("slot_used", "v_tile0", "rot_ready", "scores_ready", "transposed", "pv_done",
                             "ssq_ready", "r_ready", "mixt_ready"))
        hi_done, exp_done, pt_ready, h_hi_done, branch_sq, mix_hi_done, affine_done, silu_done, act_hi_done = (
            sem(n) for n in ("hi_done", "exp_done", "pt_ready", "h_hi_done", "branch_sq", "mix_hi_done",
                             "affine_done", "silu_done", "act_hi_done"))
        split_done, rot_read, rot_done, masked, maxed, den_done, recip_done, mixed_done = (
            sem(n) for n in ("split_done", "rot_read", "rot_done", "masked", "maxed", "den_done", "recip_done",
                             "mixed_done"))
        ms_done, diag_done, h_done, branch_ms_done, branch_scaled, tap_done = (
            sem(n) for n in ("ms_done", "diag_done", "h_done", "branch_ms_done", "branch_scaled", "tap_done"))
        cos_done, bias_ready, sq_done, sum_done, r_tok_done, branch_r_done, h_lo_done, prod_done, act_lo_done = (
            sem(n) for n in ("cos_done", "bias_ready", "sq_done", "sum_done", "r_tok_done", "branch_r_done",
                             "h_lo_done", "prod_done", "act_lo_done"))
        half_set, zeros_set, mask_begun = sem("half_set"), sem("zeros_set"), sem("mask_begun")
        acc_free = [sem("acc_free0"), sem("acc_free1")]

        def par_col(l, col):
            return par[:, bass.ds(l * NPAR + col, 1)]

        block = ctx.enter_context(nc.Block())

        @block.sync
        def _(sp):
            sp.dma_start(x[:], xT).then_inc(x_landed, 16)
            sp.dma_start(par[:], params).then_inc(par_landed, 16)
            sp.dma_start(con[:, O_ID:O_MASK], consts[:, O_ID:O_MASK]).then_inc(id_landed, 16)

            def load(g, s, src, cols):
                sp.wait_ge(split_done, RING * g + s + 1)
                sp.dma_start(w_raw[:, s, 0:cols], src).then_inc(landed[s], 16)

            with sp.Fori(0, DEPTH) as l:
                with sp.Fori(0, MAIN) as i:
                    for s in range(RING):
                        load(l * GROUPS + i, s, w_main[bass.ds(l * MAIN + i, 1), s].rearrange("a p c -> (a p) c"), PIECE)
                with sp.Fori(0, QUARTERS) as q:
                    with sp.Fori(0, G_UP) as i:
                        for s in range(RING):
                            load(l * GROUPS + q * G_QUARTER + i + G_FFN, s,
                                 w_up[bass.ds(l * FC + q * FQ + i, 1), s].rearrange("a p c -> (a p) c"), PIECE)
                    with sp.Fori(0, G_DOWN) as i:
                        for s in range(RING):
                            load(l * GROUPS + q * G_QUARTER + i + (G_FFN + G_UP), s,
                                 w_down[bass.ds(l * (QUARTERS * G_DOWN) + q * G_DOWN + i, 1), s].rearrange("a p c -> (a p) c"),
                                 PIECE_DOWN)
            for c in range(0, KC, 4):
                sp.wait_ge(h_done, DEPTH * 2 * KC + c + 4)
                sp.dma_start(outT[:, c:c + 4], h_full[:, c:c + 4]).then_inc(stored, 16)
            sp.wait_ge(stored, 16 * KC // 4)

        @block.tensor
        def _(pe):
            def mm3(out, hi, lo, start, stop, stationary_hi, stationary_lo):
                pe.matmul(out, stationary_hi, hi, start=start, stop=False)
                pe.matmul(out, stationary_hi, lo, start=False, stop=False)
                return pe.matmul(out, stationary_lo, hi, start=False, stop=stop)

            def piece_split(g, s):
                pe.wait_ge(split_done, RING * g + s + (SEED_SLOT + 1))

            def acc_taken(l, rnd, b):
                pe.wait_ge(acc_free[b], l * ROUNDS + rnd + SEED_ACC)

            def chunk(l, g, s0, rnd, b, k_ready=None):
                acc_taken(l, rnd, b)
                for k in range(KC):
                    s, kk = s0 + k // 8, k % 8
                    if kk == 0:
                        piece_split(g, s)
                    if k_ready:
                        k_ready(k)
                    w = slice(kk * P, (kk + 1) * P)
                    last = mm3(acc[b][:, 0:T], h_hi[:, k], h_lo[:, k], k == 0, k == KC - 1, w_hi[s][:, w], w_lo[s][:, w])
                    if kk == 7:
                        last.then_inc(slot_used, 1)

            def norm(n):
                for t in range(TT):
                    last = pe.matmul(aux[:, T + t:T + t + 1], sq_sum[:, t * P:(t + 1) * P], ones[:, 0:1],
                                     start=True, stop=True)
                last.then_inc(ssq_ready, 1)
                for t in range(TT):
                    pe.wait_ge(diag_done, 2 * n + t + 1)
                    last = pe.matmul(aux[:, t * P:(t + 1) * P], ones, diag[:, t], start=True, stop=True)
                last.then_inc(r_ready, 1)

            def rotate(l, i, b):
                pe.wait_ge(acc_free[b], l * ROUNDS + i + (R_PROJ + SEED_ACC + 1))
                pe.wait_ge(rot_read, l * ROT + 2 * i + (b + SEED_ROT_READ))
                pe.matmul(aux[:, 0:T], rot_m, raw[b][:], start=True, stop=True).then_inc(rot_ready, 1)

            def scores(l, pair):
                for hh in range(2):
                    pe.wait_ge(masked, l * (2 * PAIRS) + 2 * pair + (hh - 1 + SEED_HEAD))
                    rows = slice(hh * HD, (hh + 1) * HD)
                    for t in range(TT):
                        last = pe.matmul(scores_ps[hh][:, t * T:(t + 1) * T], q_sb[rows, t * P:(t + 1) * P],
                                         k_sb[rows, :], start=True, stop=True)
                    last.then_inc(scores_ready, 1)

            def transposes(l, pair):
                for hh in range(2):
                    pe.wait_ge(exp_done, l * (2 * PAIRS) + 2 * pair + (hh + 1))
                    pe.wait_ge(pt_ready, l * (2 * PAIRS) + 2 * pair + (hh - 1 + SEED_HEAD))
                    for kb in range(TT):
                        for t in range(TT):
                            last = pe.transpose(pt_ps[hh][:, kb * T + t * P:kb * T + (t + 1) * P],
                                                s_sb[:, hh, t * T + kb * P:t * T + (kb + 1) * P], ident)
                    last.then_inc(transposed, 1)

            def values(l, pair, vcol):
                pe.wait_ge(mixed_done, l * PAIRS + pair + SEED_PAIR)
                for hh in range(2):
                    pe.wait_ge(pt_ready, l * (2 * PAIRS) + 2 * pair + (hh + 1 + SEED_HEAD))
                    for t in range(TT):
                        for kb in range(TT):
                            last = pe.matmul(o_ps[:, (hh * TT + t) * HD:(hh * TT + t + 1) * HD],
                                             pt_sb[:, hh, kb * T + t * P:kb * T + (t + 1) * P],
                                             v[:, kb, bass.ds(vcol + hh * HD, HD)], start=kb == 0, stop=kb == TT - 1)
                last.then_inc(pv_done, 1)

            def mix_t(l, c):
                acc_taken(l, R_MIX + c // 2, c % 2)
                for t in range(TT):
                    last = pe.transpose(acc[c % 2][:, t * P:(t + 1) * P], mixed[:, t, c * P:(c + 1) * P], ident)
                last.then_inc(mixt_ready, 1)

            pe.wait_ge(id_landed, 16)
            with pe.Fori(0, DEPTH) as l:
                lg = l * GROUPS
                pe.wait_ge(sum_done, l * (5 * (KC + 1)) + (KC + 1))
                norm(2 * l)
                with pe.Fori(0, NVB) as blk:
                    for half in range(2):
                        for s in range(RING):
                            piece_split(lg + 2 * blk + half, s)
                            for t in range(TT):
                                if half == 0 and s == 0:
                                    acc_taken(l, blk, t)
                                for kk in range(2):
                                    k = half * 8 + s * 2 + kk
                                    if t == 0:
                                        pe.wait_ge(h_lo_done, l * (2 * KC) + (k + 1))
                                    cols = slice(kk * 512, (kk + 1) * 512)
                                    tok = slice(t * P, (t + 1) * P)
                                    pe.matmul(acc[t][:], h_hi[:, k, tok], w_hi[s][:, cols], start=k == 0, stop=False)
                                    pe.matmul(acc[t][:], h_hi[:, k, tok], w_lo[s][:, cols], start=False, stop=False)
                                    last = pe.matmul(acc[t][:], h_lo[:, k, tok], w_hi[s][:, cols], start=False,
                                                     stop=k == KC - 1)
                                if k == KC - 1 and t == 0:
                                    last.then_inc(v_tile0, 1)
                            last.then_inc(slot_used, 1)

                pe.wait_ge(con_landed, 16)
                def step_a(i, pairs_before):
                    chunk(l, lg + i + G_PROJ, 0, i + R_PROJ, 0)
                    if pairs_before >= 1:
                        rotate(l, i - 1, 1)
                    if pairs_before >= 2:
                        transposes(l, i - 2)
                    chunk(l, lg + i + G_PROJ, 2, i + R_PROJ, 1)
                    if pairs_before >= 2:
                        values(l, i - 2, (i - 2) * P)
                    if pairs_before >= 1:
                        pe.wait_ge(rot_done, l * ROT + 2 * i + SEED_ROT)
                        scores(l, i - 1)
                    rotate(l, i, 0)

                step_a(0, 0)
                step_a(1, 1)
                with pe.Fori(2, PA) as i:
                    step_a(i, 2)

                chunk(l, lg + G_PROJ + PA, 0, R_PROJ + PA, 0)
                rotate(l, PA - 1, 1)
                transposes(l, PA - 2)
                chunk(l, lg + G_PROJ + PA, 2, R_PROJ + PA, 1)
                values(l, PA - 2, (PA - 2) * P)
                pe.wait_ge(rot_done, l * ROT + 2 * PA + SEED_ROT)
                scores(l, PA - 1)
                rotate(l, PA, 0)
                rotate(l, PA, 1)
                for j in range(1, PB):
                    r = 2 * PA + 1 + j
                    pair = PA + j
                    chunk(l, lg + G_PROJ + r // 2, 2 * (r % 2), R_PROJ + r // 2, r % 2)
                    transposes(l, pair - 2)
                    pe.wait_ge(rot_done, l * ROT + r + SEED_ROT)
                    scores(l, pair - 1)
                    rotate(l, r // 2, r % 2)
                    values(l, pair - 2, (PA - 1) * P if j == 1 else WA)

                def step_c(i):
                    pair, at = PA + PB + i, PA + 3 + i
                    chunk(l, lg + G_PROJ + at, 0, R_PROJ + at, 0)
                    transposes(l, pair - 2)
                    if i == 0:
                        pe.wait_ge(rot_done, l * ROT + ROT + SEED_ROT)
                    else:
                        pe.wait_ge(acc_free[0], l * ROUNDS + (R_PROJ + at + SEED_ACC))
                        pe.wait_ge(acc_free[1], l * ROUNDS + (R_PROJ + at + SEED_ACC))
                    scores(l, pair - 1)
                    chunk(l, lg + G_PROJ + at, 2, R_PROJ + at, 1)
                    values(l, pair - 2, WA if i < 2 else WA + WKV + (i - 2) * P)

                for i in range(PC):
                    step_c(i)

                transposes(l, PAIRS - 2)
                acc_taken(l, R_MIX, 0)
                acc_taken(l, R_MIX, 1)
                scores(l, PAIRS - 1)
                values(l, PAIRS - 2, WA + WKV + (PC - 2) * P)
                pe.wait_ge(branch_scaled, 3 * l + 1)
                for c in range(PA):
                    mix_t(l, c)
                transposes(l, PAIRS - 1)
                pe.wait_ge(branch_scaled, 3 * l + 2)
                for c in range(PA, PA + 3):
                    mix_t(l, c)
                values(l, PAIRS - 1, WA + WKV + (PC - 1) * P)
                for c in range(PA + 3, PA + PB):
                    mix_t(l, c)
                pe.wait_ge(branch_scaled, 3 * l + 3)
                for c in range(PA + PB, KC):
                    mix_t(l, c)

                def mix_ready(k):
                    pe.wait_ge(acc_free[k % 2], l * ROUNDS + (R_MIX + k // 2 + SEED_ACC + 1))

                chunk(l, lg + G_OUT, 0, R_OUT, 0, mix_ready)
                chunk(l, lg + G_OUT, 2, R_OUT, 1)
                with pe.Fori(1, KC // 2) as i:
                    chunk(l, lg + i + G_OUT, 0, i + R_OUT, 0)
                    chunk(l, lg + i + G_OUT, 2, i + R_OUT, 1)

                pe.wait_ge(sum_done, l * (5 * (KC + 1)) + 2 * (KC + 1))
                norm(2 * l + 1)

                def h_ready(k):
                    pe.wait_ge(h_lo_done, l * (2 * KC) + (KC + k + 1))

                with pe.Fori(0, QUARTERS) as q:
                    g0, r0 = lg + q * G_QUARTER, q * R_QUARTER
                    chunk(l, g0 + G_FFN, 0, r0 + R_FFN, 0, h_ready)
                    chunk(l, g0 + G_FFN, 2, r0 + R_FFN, 1)
                    with pe.Fori(1, FQ) as j:
                        chunk(l, g0 + j + G_FFN, 0, r0 + j + R_FFN, 0)
                        chunk(l, g0 + j + G_FFN, 2, r0 + j + R_FFN, 1)

                    def down(i, first):
                        for s in range(RING):
                            acc_taken(l, r0 + 2 * i + (R_FFN + FQ + s // 2), s % 2)
                            piece_split(g0 + i + (G_FFN + G_UP), s)
                            for k in range(FQ):
                                if first and s == 0:
                                    pe.wait_ge(act_lo_done, l * FC + q * FQ + (k + 1 + SEED_PROD))
                                w = slice(k * P, (k + 1) * P)
                                last = mm3(acc[s % 2][:, 0:T], act_hi[:, k], act_lo[:, k], k == 0, k == FQ - 1,
                                           w_hi[s][:, w], w_lo[s][:, w])
                            last.then_inc(slot_used, 1)

                    down(0, True)
                    with pe.Fori(1, G_DOWN) as i:
                        down(i, False)
            pe.wait_ge(sum_done, DEPTH * 5 * (KC + 1) + (KC + 1))
            norm(2 * DEPTH)

        @block.scalar
        def _(act):
            def hi(g, s, cols=PIECE):
                act.wait_ge(landed[s], 16 * g + 16)
                act.wait_ge(slot_used, RING * g + s + 1)
                act.activation(w_hi[s][:, 0:cols], w_raw[:, s, 0:cols], ACT.Copy).then_inc(hi_done, 1)

            def chunk_ready(g, s):
                act.wait_ge(slot_used, RING * g + s + (SEED_SLOT + 1))

            def norm(n):
                for c in range(KC):
                    act.wait_ge(h_done, n * KC + (c + 1))
                    act.activation(h_hi[:, c], h_full[:, c], ACT.Copy).then_inc(h_hi_done, 1)

            def copy_raw(l, i, b, is_q):
                chunk_ready(l * GROUPS + i + G_PROJ, 1 + 2 * b)
                act.wait_ge(rot_done, l * ROT + 2 * i + (b - 1 + SEED_ROT))
                act.activation(raw[b][:], acc[b][:, 0:T], ACT.Copy,
                               scale=HD ** -0.5 if is_q else 1.0).then_inc(acc_free[b], 1)

            def copy_c(l, i, b):
                chunk_ready(l * GROUPS + (G_PROJ + PA + 3 + i), 1 + 2 * b)
                act.wait_ge(scores_ready, l * (2 * PAIRS) + 2 * (PA + PB + i) + SEED_SCORES)
                act.activation((k_sb if b else q_sb)[:], acc[b][:, 0:T], ACT.Copy,
                               scale=1.0 if b else HD ** -0.5).then_inc(acc_free[b], 1)

            def copy_pt(l, pair):
                for hh in range(2):
                    act.wait_ge(transposed, l * (2 * PAIRS) + 2 * pair + (hh + 1 + SEED_HEAD))
                    act.wait_ge(pv_done, l * PAIRS + pair + SEED_PAIR)
                    act.activation(pt_sb[:, hh], pt_ps[hh][:], ACT.Copy).then_inc(pt_ready, 1)

            def exps(l, pair, sink=None):
                act.wait_ge(recip_done, l * PAIRS + pair + SEED_PAIR)
                for hh in range(2):
                    act.wait_ge(maxed, l * (2 * PAIRS) + 2 * pair + (hh + 1))
                    if sink is not None:
                        act.activation(esink[:, 2 * hh:2 * hh + 2], nmx[:, 2 * hh:2 * hh + 2], ACT.Exp,
                                       bias=par_col(l, O_SINK + 2 * sink + hh))
                    for t in range(TT):
                        at = slice(t * T, (t + 1) * T)
                        last = act.activation(s_sb[:, hh, at], s_sb[:, hh, at], ACT.Exp,
                                              bias=nmx[:, 2 * hh + t:2 * hh + t + 1],
                                              accum_out=den[:, 2 * hh + t:2 * hh + t + 1])
                    last.then_inc(exp_done, 1)

            def branch_squares(l, br):
                o, w = BRANCHES[br]
                last_pair = (PA, PA + PB, PAIRS)[br]
                act.wait_ge(mixed_done, l * PAIRS + (last_pair + SEED_PAIR))
                for t in range(TT):
                    act.wait_ge(branch_sq, 3 * TT * l + (TT * br + t + SEED_SQ))
                    act.activation(junk[:, 0:w], mixed[:, t, o:o + w], ACT.Square,
                                   accum_out=branch_ssq[:, br, t:t + 1]).then_inc(branch_sq, 1)

            def mix_hi(l, c):
                act.wait_ge(mixt_ready, l * KC + (c + 1))
                act.activation(h_hi[:, c], acc[c % 2][:, 0:T], ACT.Copy,
                               scale=par_col(l, O_MIX + c)).then_inc(mix_hi_done, 1)

            act.wait_ge(half_set, 1)
            act.wait_ge(x_landed, 16)
            for t in range(4):
                tok = slice(t * T // 4, (t + 1) * T // 4)
                act.activation(h_full[:, :, tok], x[:, :, tok], ACT.Square).then_inc(sq_done, KC // 4)
            for s in range(RING):
                hi(0, s)
            act.wait_ge(par_landed, 16)
            with act.Fori(0, DEPTH) as l:
                lg = l * GROUPS
                norm(2 * l)
                with act.Fori(0, NVB) as blk:
                    for s in range(RING):
                        hi(lg + 2 * blk + 1, s)
                    for s in range(RING - 1):
                        hi(lg + 2 * blk + 2, s)
                    act.wait_ge(v_tile0, NVB * l + blk + 1)
                    act.activation(v[:, 0, bass.ds(blk * 512, 512)], acc[0][:], ACT.Copy).then_inc(acc_free[0], 1)
                    hi(lg + 2 * blk + 2, RING - 1)
                    act.activation(v[:, 1, bass.ds(blk * 512, 512)], acc[1][:], ACT.Copy).then_inc(acc_free[1], 1)

                def step_a(i, pairs_before):
                    g = lg + i + (G_PROJ + 1)
                    hi(g, 0)
                    hi(g, 1)
                    copy_raw(l, i, 0, True)
                    if pairs_before >= 2:
                        copy_pt(l, i - 2)
                    hi(g, 2)
                    hi(g, 3)
                    copy_raw(l, i, 1, False)
                    if pairs_before >= 1:
                        exps(l, i - 1)

                step_a(0, 0)
                step_a(1, 1)
                with act.Fori(2, PA) as i:
                    step_a(i, 2)
                g = lg + (G_PROJ + PA + 1)
                hi(g, 0)
                hi(g, 1)
                copy_raw(l, PA, 0, False)
                copy_pt(l, PA - 2)
                hi(g, 2)
                hi(g, 3)
                copy_raw(l, PA, 1, True)
                exps(l, PA - 1)
                for j in range(1, PB):
                    r = 2 * PA + 1 + j
                    g = lg + (G_PROJ + r // 2 + 1)
                    hi(g, 2 * (r % 2))
                    hi(g, 2 * (r % 2) + 1)
                    copy_raw(l, r // 2, r % 2, True)
                    copy_pt(l, PA + j - 2)
                    exps(l, PA + j - 1, sink=j - 1)
                for i in range(PC):
                    g = lg + (G_PROJ + PA + 3 + i + 1)
                    pair = PA + PB + i
                    hi(g, 0)
                    hi(g, 1)
                    copy_c(l, i, 0)
                    copy_pt(l, pair - 2)
                    hi(g, 2)
                    exps(l, pair - 1, sink=PB - 1 if i == 0 else None)
                    hi(g, 3)
                    copy_c(l, i, 1)
                    if i == 1:
                        branch_squares(l, 0)
                    if i == 3:
                        branch_squares(l, 1)
                copy_pt(l, PAIRS - 2)
                exps(l, PAIRS - 1)
                for c in range(PA):
                    mix_hi(l, c)
                copy_pt(l, PAIRS - 1)
                for c in range(PA, PA + PB):
                    mix_hi(l, c)
                branch_squares(l, 2)
                for c in range(PA + PB, KC):
                    mix_hi(l, c)
                act.activation(silu_first[:], minus_half[:], ACT.Silu)
                with act.Fori(0, KC // 2) as i:
                    for s in range(RING):
                        hi(lg + i + (G_OUT + 1), s)
                norm(2 * l + 1)

                with act.Fori(0, QUARTERS) as q:
                    g0 = lg + q * G_QUARTER

                    def up(j, cols):
                        g = g0 + j + (G_FFN + 1)
                        f = q * FQ + j
                        col = l * NPAR + 8 * f
                        hi(g, 0, cols)
                        hi(g, 1, cols)
                        chunk_ready(g - 1, 1)
                        act.activation(gate[:], acc[0][:, 0:T], ACT.Identity,
                                       scale=par[:, bass.ds(col + (O_CONV + 1), 1)],
                                       bias=par[:, bass.ds(col + (O_CONV + 3), 1)]).then_inc(affine_done, 1)
                        hi(g, 2, cols)
                        act.wait_ge(acc_free[0], l * ROUNDS + q * R_QUARTER + j + (R_FFN + SEED_ACC + 1))
                        act.wait_ge(prod_done, l * FC + f + SEED_PROD)
                        act.activation(silu[:], gate[:], ACT.Silu).then_inc(silu_done, 1)
                        hi(g, 3, cols)
                        chunk_ready(g - 1, 3)
                        act.activation(value[:], acc[1][:, 0:T], ACT.Identity,
                                       scale=par[:, bass.ds(col + (O_CONV + 5), 1)],
                                       bias=par[:, bass.ds(col + (O_CONV + 7), 1)]).then_inc(affine_done, 1)
                        act.wait_ge(prod_done, l * FC + f + (SEED_PROD + 1))
                        act.activation(act_hi[:, bass.ds(j, 1)].rearrange("p a t -> p (a t)"), prod[:],
                                       ACT.Copy).then_inc(act_hi_done, 1)

                    with act.Fori(0, FQ - 1) as j:
                        up(j, PIECE)
                    up(FQ - 1, PIECE_DOWN)
                    with act.Fori(0, G_DOWN - 1) as i:
                        for s in range(RING):
                            hi(g0 + i + (G_FFN + G_UP + 1), s, PIECE_DOWN)
                    with act.If(g0 + (G_FFN + G_QUARTER) < DEPTH * GROUPS):
                        for s in range(RING):
                            hi(g0 + (G_FFN + G_QUARTER), s)

        @block.vector
        def _(dve):
            def lo(g, s, cols=PIECE):
                dve.wait_ge(hi_done, RING * g + s + 1)
                dve.tensor_tensor(w_lo[s][:, 0:cols], w_raw[:, s, 0:cols], w_hi[s][:, 0:cols].bitcast(F32),
                                  ALU.subtract).then_inc(split_done, 1)

            def norm(n, gains):
                dve.wait_ge(ssq_ready, n + 1)
                dve.tensor_scalar(ms[:], aux[:, T:T + TT], 1.0 / D, EPS, ALU.mult, ALU.add).then_inc(ms_done, 1)
                dve.wait_ge(r_tok_done, n + 1)
                for t in range(TT):
                    dve.tensor_scalar(diag[:, t], ident, r_tok[:, t:t + 1], None, ALU.mult).then_inc(diag_done, 1)
                dve.wait_ge(r_ready, n + 1)
                for c in range(KC):
                    dve.scalar_tensor_tensor(h_full[:, c], x[:, c], gains(c), aux[:, 0:T], ALU.mult,
                                             ALU.mult).then_inc(h_done, 1)

            def rotated(l, i, b, pair, is_q):
                dve.wait_ge(rot_ready, l * ROT + 2 * i + (b + 1))
                dve.wait_ge(rot_done, l * ROT + 2 * i + (b + SEED_ROT))
                dve.tensor_tensor(rot_sin[:], aux[:, 0:T], sin, ALU.mult).then_inc(rot_read, 1)
                dve.wait_ge(rot_read, l * ROT + 2 * i + (b + SEED_ROT_READ + 1))
                dve.wait_ge(cos_done, l * ROT + 2 * i + (b + 1))
                dve.wait_ge(scores_ready, l * (2 * PAIRS) + 2 * pair + SEED_SCORES)
                dve.tensor_tensor((q_sb if is_q else k_sb)[:], rot_sin[:], rot_cos[:], ALU.add).then_inc(rot_done, 1)

            def mask(l, pair, masks, sink=None):
                for hh in range(2):
                    dve.wait_ge(scores_ready, l * (2 * PAIRS) + 2 * pair + (hh + 1 + SEED_SCORES))
                    dve.wait_ge(transposed, l * (2 * PAIRS) + 2 * pair + (hh - 1 + SEED_HEAD))
                    dve.sem_inc(mask_begun, 1)
                    for t in range(TT):
                        at = slice(t * T, (t + 1) * T)
                        last = dve.tensor_tensor_reduce(s_sb[:, hh, at], scores_ps[hh][:, at], masks[hh][:, at], 1.0,
                                                        -3e38, ALU.add, ALU.max, mx[:, 2 * hh + t:2 * hh + t + 1])
                    last.then_inc(masked, 1)
                    dve.wait_ge(masked, l * (2 * PAIRS) + 2 * pair + (hh + 1 + SEED_HEAD))
                    if sink is None:
                        last = dve.tensor_scalar(nmx[:, 2 * hh:2 * hh + 2], mx[:, 2 * hh:2 * hh + 2], -1.0, None, ALU.mult)
                    else:
                        last = dve.tensor_scalar(nmx[:, 2 * hh:2 * hh + 2], mx[:, 2 * hh:2 * hh + 2],
                                                 par_col(l, O_SINK + 2 * sink + hh), -1.0, ALU.max, ALU.mult)
                    last.then_inc(maxed, 1)

            def recip(l, pair, sink=None):
                dve.wait_ge(exp_done, l * (2 * PAIRS) + 2 * pair + 2)
                total = den
                if sink is not None:
                    dve.tensor_tensor(den_all[:], den[:], esink[:], ALU.add).then_inc(den_done, 1)
                    dve.wait_ge(den_done, PB * l + (sink + 1))
                    total = den_all
                dve.wait_ge(mixed_done, l * PAIRS + pair + SEED_PAIR)
                dve.reciprocal(rden[:], total[:]).then_inc(recip_done, 1)

            def outputs(l, pair):
                dve.wait_ge(recip_done, l * PAIRS + pair + (1 + SEED_PAIR))
                dve.wait_ge(pv_done, l * PAIRS + pair + (1 + SEED_PAIR))
                to = mixed[:, :, bass.ds(pair * P, P)].rearrange("p t (h d) -> p h t d", h=2)
                dve.tensor_tensor(to, o_ps[:, 0:2 * TT * HD].rearrange("p (h t d) -> p h t d", h=2, t=TT),
                                  rden[:].rearrange("p (h t) -> p h t", h=2).unsqueeze(3).to_broadcast([P, 2, TT, HD]),
                                  ALU.mult).then_inc(mixed_done, 1)

            def branch_norm(l, br):
                o, w = BRANCHES[br]
                dve.wait_ge(branch_sq, 3 * TT * l + (TT * br + TT + SEED_SQ))
                dve.tensor_scalar(branch_ms[:, br], branch_ssq[:, br], 1.0 / w, EPS, ALU.mult,
                                  ALU.add).then_inc(branch_ms_done, 1)
                dve.wait_ge(branch_r_done, 3 * l + (br + 1))
                for t in range(TT):
                    last = dve.tensor_scalar(mixed[:, t, o:o + w], mixed[:, t, o:o + w], branch_r[:, br, t:t + 1], None,
                                             ALU.mult)
                last.then_inc(branch_scaled, 1)

            def mix_lo(l, c):
                dve.wait_ge(mix_hi_done, l * KC + (c + 1))
                dve.scalar_tensor_tensor(h_lo[:, c], acc[c % 2][:, 0:T], par_col(l, O_MIX + c),
                                         h_hi[:, c].bitcast(F32), ALU.mult, ALU.subtract).then_inc(acc_free[c % 2], 1)

            def add_to_x(g, s, m, b, squared):
                dve.wait_ge(slot_used, RING * g + s + (SEED_SLOT + 1))
                dve.wait_ge(sq_done, squared)
                xm = x[:, bass.ds(m, 1)].rearrange("p a t -> p (a t)")
                dve.tensor_tensor(xm, acc[b][:, 0:T], xm, ALU.add).then_inc(acc_free[b], 1)

            for s_, n in ((slot_used, SEED_SLOT), (split_done, SEED_SLOT), (acc_free[0], SEED_ACC),
                          (acc_free[1], SEED_ACC), (scores_ready, SEED_SCORES), (transposed, SEED_HEAD),
                          (masked, SEED_HEAD), (pt_ready, SEED_HEAD), (pv_done, SEED_PAIR), (recip_done, SEED_PAIR),
                          (mixed_done, SEED_PAIR), (rot_done, SEED_ROT), (rot_read, SEED_ROT_READ),
                          (prod_done, SEED_PROD), (act_lo_done, SEED_PROD), (branch_sq, SEED_SQ)):
                dve.sem_inc(s_, n)
            dve.wait_ge(id_landed, 16)
            dve.wait_ge(par_landed, 16)
            for t in range(4):
                dve.wait_ge(sq_done, (t + 1) * KC // 4)
                tok = slice(t * T // 4, (t + 1) * T // 4)
                dve.tensor_reduce(sq_sum[:, tok], h_full[:, :, tok].rearrange("p k t -> p t k"), AX.X,
                                  ALU.add).then_inc(sum_done, KC // 4 + t // 3)
            for s in range(RING):
                lo(0, s)
            with dve.Fori(0, DEPTH) as l:
                lg = l * GROUPS
                norm(2 * l, lambda c: par_col(l, O_LN1 + c))
                with dve.Fori(0, 2 * NVB) as i:
                    for s in range(RING):
                        lo(lg + i + 1, s)

                dve.wait_ge(con_landed, 16)
                dve.wait_ge(mask_landed, 16)
                masks_a, masks_b = (mask_a, mask_a), (mask_b, mask_b)

                def step_a(i, pairs_before):
                    g = lg + i + (G_PROJ + 1)
                    lo(g, 0)
                    if pairs_before >= 2:
                        recip(l, i - 2)
                    if pairs_before >= 1:
                        rotated(l, i - 1, 1, i - 1, False)
                    lo(g, 1)
                    lo(g, 2)
                    lo(g, 3)
                    if pairs_before >= 2:
                        outputs(l, i - 2)
                    if pairs_before >= 1:
                        mask(l, i - 1, masks_a)
                    rotated(l, i, 0, i, True)

                step_a(0, 0)
                step_a(1, 1)
                with dve.Fori(2, PA) as i:
                    step_a(i, 2)
                g = lg + (G_PROJ + PA + 1)
                lo(g, 0)
                recip(l, PA - 2)
                rotated(l, PA - 1, 1, PA - 1, False)
                lo(g, 1)
                lo(g, 2)
                lo(g, 3)
                outputs(l, PA - 2)
                mask(l, PA - 1, masks_a)
                rotated(l, PA, 0, PA, False)
                rotated(l, PA, 1, PA, True)
                for j in range(1, PB):
                    r = 2 * PA + 1 + j
                    g = lg + (G_PROJ + r // 2 + 1)
                    lo(g, 2 * (r % 2))
                    lo(g, 2 * (r % 2) + 1)
                    recip(l, PA + j - 2, sink=j - 2 if j >= 2 else None)
                    mask(l, PA + j - 1, masks_b, sink=j - 1)
                    rotated(l, r // 2, r % 2, PA + j, True)
                    outputs(l, PA + j - 2)
                for i in range(PC):
                    g = lg + (G_PROJ + PA + 3 + i + 1)
                    pair = PA + PB + i
                    if i == 1:
                        dve.wait_ge(bias_ready, HC * (l + 1))
                    recip(l, pair - 2, sink=PB - 2 + i if i < 2 else None)
                    lo(g, 0)
                    lo(g, 1)
                    if i == 0:
                        mask(l, pair - 1, masks_b, sink=PB - 1)
                    else:
                        mask(l, pair - 1, (bias[:, 2 * i - 2], bias[:, 2 * i - 1]))
                    lo(g, 2)
                    lo(g, 3)
                    outputs(l, pair - 2)
                    if i == 2:
                        branch_norm(l, 0)
                    if i == 4:
                        branch_norm(l, 1)
                recip(l, PAIRS - 2)
                mask(l, PAIRS - 1, (bias[:, HC - 2], bias[:, HC - 1]))
                outputs(l, PAIRS - 2)
                for c in range(PA):
                    mix_lo(l, c)
                recip(l, PAIRS - 1)
                for c in range(PA, PA + 3):
                    mix_lo(l, c)
                outputs(l, PAIRS - 1)
                for c in range(PA + 3, PA + PB):
                    mix_lo(l, c)
                branch_norm(l, 2)
                for c in range(PA + PB, KC):
                    mix_lo(l, c)

                with dve.Fori(0, KC // 2) as i:
                    g = lg + i + G_OUT
                    for b in range(2):
                        lo(g + 1, 2 * b)
                        lo(g + 1, 2 * b + 1)
                        add_to_x(g, 1 + 2 * b, 2 * i + b, b, l * (5 * KC) + 2 * i + (b + 1))
                norm(2 * l + 1, lambda c: par_col(l, O_LN2 + c))

                with dve.Fori(0, QUARTERS) as q:
                    g0 = lg + q * G_QUARTER

                    def up(j, cols):
                        g = g0 + j + (G_FFN + 1)
                        f = q * FQ + j
                        col = l * NPAR + 8 * f
                        for b, u in ((0, gate), (1, value)):
                            lo(g, 2 * b, cols)
                            lo(g, 2 * b + 1, cols)
                            dve.wait_ge(affine_done, l * (2 * FC) + 2 * f + (b + 1))
                            dve.scalar_tensor_tensor(u[:, 1:T], acc[b][:, 0:T - 1],
                                                     par[:, bass.ds(col + (O_CONV + 4 * b), 1)], u[:, 1:T],
                                                     ALU.mult, ALU.add).then_inc(tap_done, 1)
                            dve.wait_ge(tap_done, l * (2 * FC) + 2 * f + (b + 1))
                            dve.scalar_tensor_tensor(u[:, 0:T - 1], acc[b][:, 1:T],
                                                     par[:, bass.ds(col + (O_CONV + 4 * b + 2), 1)], u[:, 0:T - 1],
                                                     ALU.mult, ALU.add).then_inc(acc_free[b], 1)

                    with dve.Fori(0, FQ - 1) as j:
                        up(j, PIECE)
                    up(FQ - 1, PIECE_DOWN)

                    def down(i, s):
                        add_to_x(g0 + i + (G_FFN + G_UP), s, 4 * i + s, s % 2,
                                 l * (5 * KC) + q * KC + 4 * i + (KC + s + 1))

                    with dve.Fori(0, G_DOWN - 1) as i:
                        for s in range(RING):
                            lo(g0 + i + (G_FFN + G_UP + 1), s, PIECE_DOWN)
                            down(i, s)
                    for s in range(RING):
                        down(G_DOWN - 1, s)
                    with dve.If(g0 + (G_FFN + G_QUARTER) < DEPTH * GROUPS):
                        for s in range(RING):
                            lo(g0 + (G_FFN + G_QUARTER), s)
            norm(2 * DEPTH, lambda c: par[:, DEPTH * NPAR + c:DEPTH * NPAR + c + 1])

        @block.gpsimd
        def _(pool):
            pool.memset(minus_half[:], -0.5).then_inc(half_set, 1)
            pool.memset(zeros[:], 0.0).then_inc(zeros_set, 1)
            pool.wait_ge(zeros_set, 1)

            def squares_begin():
                pool.tensor_tensor(sq_sum[:], zeros[:], zeros[:], ALU.add).then_inc(sum_done, 1)

            def square(n, c):
                xc = x[:, bass.ds(c, 1)].rearrange("p a t -> p (a t)")
                pool.wait_ge(sum_done, n * (KC + 1) + c + 1)
                pool.tensor_tensor(sq[:], xc, xc, ALU.mult).then_inc(sq_done, 1)
                pool.wait_ge(sq_done, n * KC + c + 1)
                pool.tensor_tensor(sq_sum[:], sq_sum[:], sq[:], ALU.add).then_inc(sum_done, 1)

            def norm(n):
                pool.wait_ge(ms_done, n + 1)
                pool.tensor_tensor(r_tok[:], ms[:], minus_half[:], ALU.pow).then_inc(r_tok_done, 1)

            def h_los(n):
                for c in range(KC):
                    pool.wait_ge(h_hi_done, n * KC + (c + 1))
                    pool.tensor_tensor(h_lo[:, c], h_full[:, c], h_hi[:, c].bitcast(F32),
                                       ALU.subtract).then_inc(h_lo_done, 1)

            def cos_product(l, i, b):
                pool.wait_ge(acc_free[b], l * ROUNDS + i + (R_PROJ + SEED_ACC + 1))
                pool.wait_ge(rot_done, l * ROT + 2 * i + (b + SEED_ROT))
                pool.tensor_tensor(rot_cos[:], raw[b][:], cos, ALU.mult).then_inc(cos_done, 1)

            def branch_rsqrt(l, br):
                pool.wait_ge(branch_ms_done, 3 * l + (br + 1))
                pool.tensor_tensor(branch_r[:, br], branch_ms[:, br], minus_half[:], ALU.pow).then_inc(branch_r_done, 1)

            pool.wait_ge(half_set, 1)
            pool.wait_ge(x_landed, 16)
            pool.dma_start(con[:, 0:O_ID], consts[:, 0:O_ID]).then_inc(con_landed, 16)
            pool.dma_start(con[:, O_MASK:NCONST], consts[:, O_MASK:NCONST]).then_inc(mask_landed, 16)
            with pool.Fori(0, DEPTH) as l:
                pool.dma_start(bias[:], bias_c[bass.ds(l, 1)].rearrange("a p h c -> (a p) h c")).then_inc(bias_landed, 16)
                norm(2 * l)
                h_los(2 * l)
                pool.wait_ge(con_landed, 16)
                pool.wait_ge(mask_landed, 16)
                pool.wait_ge(bias_landed, 16 * l + 16)
                for hc in range(HC):
                    pool.tensor_tensor(bias[:, hc], bias[:, hc], mask_c, ALU.add).then_inc(bias_ready, 1)
                with pool.Fori(0, ROT // 2) as i:
                    cos_product(l, i, 0)
                    cos_product(l, i, 1)
                for br in range(3):
                    branch_rsqrt(l, br)
                pool.wait_ge(ssq_ready, 2 * l + 1)
                squares_begin()
                with pool.Fori(0, KC // 2) as i:
                    for b in range(2):
                        pool.wait_ge(acc_free[b], l * ROUNDS + i + (R_OUT + SEED_ACC + 1))
                        square(5 * l + 1, 2 * i + b)
                norm(2 * l + 1)
                h_los(2 * l + 1)
                with pool.Fori(0, QUARTERS) as q:
                    def ffn(j):
                        f = q * FQ + j
                        pool.wait_ge(silu_done, l * FC + f + 1)
                        pool.wait_ge(acc_free[1], l * ROUNDS + q * R_QUARTER + j + (R_FFN + SEED_ACC + 1))
                        pool.wait_ge(act_lo_done, l * FC + f + SEED_PROD)
                        pool.tensor_tensor(prod[:], silu[:], value[:], ALU.mult).then_inc(prod_done, 1)
                        pool.wait_ge(act_hi_done, l * FC + f + 1)
                        at = bass.ds(j, 1)
                        pool.tensor_tensor(act_lo[:, at].rearrange("p a t -> p (a t)"), prod[:],
                                           act_hi[:, at].rearrange("p a t -> p (a t)").bitcast(F32),
                                           ALU.subtract).then_inc(act_lo_done, 1)

                    with pool.Fori(0, FQ) as j:
                        ffn(j)
                    pool.wait_ge(sum_done, (5 * l + q + 2) * (KC + 1))
                    pool.wait_ge(ssq_ready, 2 * l + 2)
                    squares_begin()
                    with pool.Fori(0, KC // 2) as i:
                        for b in range(2):
                            pool.wait_ge(acc_free[b], l * ROUNDS + q * R_QUARTER + i + (R_FFN + FQ + SEED_ACC + 1))
                            square(5 * l + q + 2, 2 * i + b)
            norm(2 * DEPTH)


def _constants():
    f32 = np.float32
    inv = (f32(10000.0) ** (-np.arange(0, HD, 2, dtype=f32) / f32(HD))).astype(f32)
    ang = np.arange(T, dtype=f32)[:, None] * inv[None, :]
    four = np.tile(ang.T, (4, 1))
    swap = np.zeros((P, P), f32)
    half = HD // 2
    for base in (0, HD):
        for d in range(half):
            swap[base + half + d, base + d] = -1.0
            swap[base + d, base + half + d] = 1.0
    q, k = np.arange(T)[:, None], np.arange(T)[None, :]
    times = np.zeros((T, T))
    for window, r in ((128, 1), (512, 4), (2048, 16)):
        times += (q % r == k % r) & (np.abs(q // r - k // r) <= window // (2 * r))
    m_a = np.where(times > 0, np.log(np.maximum(times, 1.0)), NEG)
    m_b = np.where(np.abs(q - k) <= 128, 0.0, NEG)
    start = np.clip(q % 64 - 8, 0, 64 - 16)
    m_c = np.where((k % 64 >= start) & (k % 64 < start + 16), 0.0, NEG)
    tiled = [m.reshape(TT, P, T).transpose(1, 0, 2).reshape(P, TT * T).astype(f32) for m in (m_a, m_b, m_c)]
    return np.ascontiguousarray(np.concatenate(
        [np.cos(four), np.sin(four), swap, np.eye(P, dtype=f32), np.ones((P, P), f32), *tiled], 1).astype(f32))


def _chunks(w):
    n = w.shape[1] // P
    return w.reshape(2, 8, P, n, P).transpose(3, 0, 2, 1, 4).reshape(n, 2, P, PIECE)


def kernel(**inputs):
    import concourse.bacc as bacc
    from concourse.bass_utils import run_bass_kernel_spmd

    a = {k: np.asarray(v_) for k, v_ in inputs.items()}
    heads_b = [j + h * PB for j in range(PB) for h in range(HKV)]
    w_main, w_up, w_down, params, biases = [], [], [], [], []
    at = np.cumsum([0, WA, WA, WA, WB, WKV, WKV, WC, WC, WC])
    row = np.arange(T)
    cols_off = np.clip(row[None, :] % 64 - row[:, None] % 64 + 15, 0, 30)
    rows_off = row[None, :] // 64 - row[:, None] // 64 + 7
    for l in range(DEPTH):
        qa, ka, va, qb, kb, vb, qc, kc, vc = (a["w_in"][l][:, at[i]:at[i + 1]] for i in range(9))
        qb = qb.reshape(D, HB, HD)[:, heads_b].reshape(D, WB)
        wv = np.concatenate([va, vb, vc], 1)
        v_pieces = wv.reshape(8, 2, P, NVB, 512).transpose(3, 0, 2, 1, 4).reshape(-1, P, PIECE)

        def by_turns(wq, wk):
            return np.stack([_chunks(wq), _chunks(wk)], 1).reshape(-1, P, PIECE)

        order = [slice(0, WA), None, slice(WA + WB, D)]
        wo = a["w_out"][l]
        wo_b = wo[WA:WA + WB].reshape(HB, HD, D)[heads_b].reshape(WB, D)
        wo = np.concatenate([wo[order[0]], wo_b, wo[order[2]]], 0)
        mg = a["mix_gain"][l]
        mg = np.concatenate([mg[:WA], mg[WA:WA + WB].reshape(HB, HD)[heads_b].reshape(-1), mg[WA + WB:]])
        w_main.append(np.concatenate([
            v_pieces, by_turns(qa, ka), _chunks(np.concatenate([kb, qb], 1)).reshape(-1, P, PIECE),
            by_turns(qc, kc), _chunks(wo).reshape(-1, P, PIECE)]).reshape(MAIN, RING, P, PIECE))
        up = a["w_up"][l]
        w_up.append(by_turns(up[:, :D_FF], up[:, D_FF:]).reshape(FC, RING, P, PIECE))
        w_down.append(a["w_down"][l].reshape(QUARTERS, FQ, P, KC, P).transpose(0, 3, 2, 1, 4)
                      .reshape(QUARTERS * G_DOWN, RING, P, PIECE_DOWN))
        conv = np.concatenate([a["conv_w"][l], a["conv_b"][l][None]], 0).reshape(4, 2, FC, P)
        params += [a["ln_attn"][l].reshape(KC, P).T, mg.reshape(KC, P).T, a["ln_ffn"][l].reshape(KC, P).T,
                   conv.transpose(3, 2, 1, 0).reshape(P, 8 * FC),
                   np.broadcast_to(a["sink_b"][l][heads_b], (P, HB))]
        rpb = a["rpb_c"][l][:, rows_off, cols_off]
        biases.append(rpb.reshape(HC, TT, P, T).transpose(2, 0, 1, 3).reshape(P, HC, TT * T))
    params.append(a["ln_final"].reshape(KC, P).T)
    arrays = {
        "in_x": a["x"][0].reshape(T, KC, P).transpose(2, 1, 0),
        "in_w_main": np.stack(w_main).reshape(DEPTH * MAIN, RING, P, PIECE),
        "in_w_up": np.stack(w_up).reshape(DEPTH * FC, RING, P, PIECE),
        "in_w_down": np.stack(w_down).reshape(DEPTH * QUARTERS * G_DOWN, RING, P, PIECE_DOWN),
        "in_bias_c": np.stack(biases),
        "in_params": np.concatenate(params, 1),
        "in_consts": _constants(),
    }
    arrays = {k: np.ascontiguousarray(v_) for k, v_ in arrays.items()}
    nc = bacc.Bacc("TRN2", target_bir_lowering=False, num_devices=1)
    args = [nc.dram_tensor(n, v_.shape, F32, kind="ExternalInput").ap() for n, v_ in arrays.items()]
    args.append(nc.dram_tensor("out_y", (P, KC, T), F32, kind="ExternalOutput").ap())
    build(nc, *args)
    r = run_bass_kernel_spmd(nc, [arrays], core_ids=[0])
    y = np.asarray(r.results[0]["out_y"])
    return y.transpose(2, 1, 0).reshape(1, T, D)
```

```python
from contextlib import ExitStack

import numpy as np
import concourse.bass as bass
from concourse import mybir

P = 128
F32 = mybir.dt.float32
F32R = mybir.dt.float32r
ALU = mybir.AluOpType
ACT = mybir.ActivationFunctionType
AX = mybir.AxisListType

DEPTH, D, T, HD, D_FF = 2, 2048, 256, 64, 5632
HA, HB, HC, HKV = 12, 10, 10, 2
WA, WB, WKV, WC = HA * HD, HB * HD, HKV * HD, HC * HD
VCOLS = WA + WKV + WC
EPS = 1e-6
NEG = -1e30

KC = D // P
TT = T // P
NVB = VCOLS // 512
FC = D_FF // P
QUARTERS = 4
FQ = FC // QUARTERS

PA, PB, PC = HA // 2, HB // 2, HC // 2
PAIRS = PA + PB + PC
ROT = 2 * PA + 1 + PB
BRANCHES = ((0, WA), (WA, WB), (WA + WB, WC))

RING = 4
PIECE = 8 * P
PIECE_DOWN = FQ * P
G_V, G_PROJ, G_OUT, G_FFN = 0, 2 * NVB, 2 * NVB + 14, 2 * NVB + 14 + KC // 2
G_UP, G_DOWN = FQ, KC // 4
G_QUARTER = G_UP + G_DOWN
GROUPS = G_FFN + QUARTERS * G_QUARTER
MAIN = G_FFN

MIX_ACC = 10
R_V, R_PROJ, R_MIX, R_OUT = 0, NVB, NVB + 14, NVB + 14 + MIX_ACC // 2
R_FFN = R_OUT + KC // 2
R_QUARTER = FQ + KC // 2
ROUNDS = R_FFN + QUARTERS * R_QUARTER

O_LN1, O_MIX, O_LN2, O_CONV, O_SINK = 0, KC, 2 * KC, 3 * KC, 3 * KC + 8 * FC
NPAR = O_SINK + HB
O_COS, O_SIN, O_ROT, O_ID, O_ONE = 0, T, 2 * T, 2 * T + P, 2 * T + 2 * P
O_MASK = 2 * T + 3 * P
NCONST = O_MASK + 3 * TT * T

SEED_SLOT = RING
SEED_ACC = 1
SEED_SCORES = 1
SEED_HEAD = 2
SEED_PAIR = 1
SEED_ROT = 2
SEED_ROT_READ = 1
SEED_PROD = 1
SEED_SQ = 1
SEED_CONV = 2


def build(nc, xT, w_main, w_up, w_down, bias_c, params, consts, outT):
    with ExitStack() as ctx:
        def sb(name, shape, dt=F32):
            return ctx.enter_context(nc.sbuf_tensor(name, shape, dt))

        def bank(name):
            return ctx.enter_context(nc.psum_tensor(name, [P, 512], F32))

        def sem(name):
            return ctx.enter_context(nc.semaphore(name))

        acc = [bank("acc0"), bank("acc1")]
        aux = bank("aux")
        scores_ps = [bank("scores0"), bank("scores1")]
        pt_ps = [bank("pt0"), bank("pt1")]
        o_ps = bank("o_ps")

        x = sb("x", [P, KC, T])
        h_hi, h_lo = sb("h_hi", [P, KC, T], F32R), sb("h_lo", [P, KC, T], F32R)
        with nc.sbuf_tensor("mixed", [P, TT, D], F32) as mixed:
            pass
        h2_hi = sb("h2_hi", [P, KC, T], F32R)
        with nc.sbuf_tensor("v", [P, TT, VCOLS], F32) as v, nc.sbuf_tensor("pt_sb", [P, 2, TT * T], F32) as pt_sb:
            pass
        h2_lo = sb("h2_lo", [P, KC, T], F32R)
        as_chunks = mixed.ap().rearrange("p t (k c) -> p (t k) c", c=T)
        w_raw = sb("w_raw", [P, RING, PIECE_DOWN])
        w_hi = [sb(f"w_hi{s}", [P, PIECE_DOWN], F32R) for s in range(RING)]
        w_lo = [sb(f"w_lo{s}", [P, PIECE_DOWN], F32R) for s in range(RING)]
        with nc.sbuf_tensor("bias", [P, HC, TT * T], F32) as bias:
            pass
        act_hi, act_lo = sb("act_hi", [P, FQ, T], F32R), sb("act_lo", [P, FQ, T], F32R)
        par = sb("par", [P, DEPTH * NPAR + KC])
        con = sb("con", [P, NCONST])
        raw = [sb("raw0", [P, T]), sb("raw1", [P, T])]
        q_sb, k_sb = sb("q_sb", [P, T]), sb("k_sb", [P, T])
        rot_sin, rot_cos = sb("rot_sin", [P, T]), sb("rot_cos", [P, T])
        with nc.sbuf_tensor("s_sb", [P, 2, TT * T], F32) as s_sb:
            pass
        gate, value = sb("gate", [P, T]), sb("value", [P, T])
        silu, prod = sb("silu", [P, T]), sb("prod", [P, T])
        junk = sb("junk", [P, WA])
        mx, nmx = sb("mx", [P, 4]), sb("nmx", [P, 4])
        den, esink, den_all, rden = (sb(n, [P, 4]) for n in ("den", "esink", "den_all", "rden"))
        branch_ssq, branch_ms, branch_r = (sb(n, [P, 4, TT]) for n in ("branch_ssq", "branch_ms", "branch_r"))
        sq, sq_sum = sb("sq", [P, T]), sb("sq_sum", [P, T])
        ms, r_tok = sb("ms", [P, TT]), sb("r_tok", [P, TT])
        r_all = sb("r_all", [P, T])
        z = [sb("z0", [P, T]), sb("z1", [P, T])]
        silu_first = sb("silu_first", [P, TT])
        minus_half, zeros = sb("minus_half", [P, TT]), sb("zeros", [P, T])
        diag = sb("diag", [P, TT, P])

        cos, sin = con[:, O_COS:O_COS + T], con[:, O_SIN:O_SIN + T]
        rot_m, ident, ones = (con[:, o:o + P] for o in (O_ROT, O_ID, O_ONE))
        mask_a, mask_b, mask_c = (con[:, O_MASK + b * TT * T:O_MASK + (b + 1) * TT * T] for b in range(3))

        landed = [sem(f"landed{s}") for s in range(RING)]
        x_landed = [sem(f"x_landed{i}") for i in range(RING)]
        par_landed, id_landed, con_landed, mask_landed, bias_landed, stored = (
            sem(n) for n in ("par_landed", "id_landed", "con_landed", "mask_landed", "bias_landed",
                             "stored"))
        slot_used, v_tile0, rot_ready, scores_ready, transposed, pv_done, ssq_ready, r_ready, mixt_ready = (
            sem(n) for n in ("slot_used", "v_tile0", "rot_ready", "scores_ready", "transposed", "pv_done",
                             "ssq_ready", "r_ready", "mixt_ready"))
        hi_done, exp_done, pt_ready, h_hi_done, branch_sq, mix_hi_done, affine_done, silu_done, act_hi_done = (
            sem(n) for n in ("hi_done", "exp_done", "pt_ready", "h_hi_done", "branch_sq", "mix_hi_done",
                             "affine_done", "silu_done", "act_hi_done"))
        split_done, rot_read, rot_done, masked, maxed, den_done, recip_done, mixed_done = (
            sem(n) for n in ("split_done", "rot_read", "rot_done", "masked", "maxed", "den_done", "recip_done",
                             "mixed_done"))
        ms_done, diag_done, r_all_done, h_lo_done, mix_lo_done, y_done = (
            sem(n) for n in ("ms_done", "diag_done", "r_all_done", "h_lo_done", "mix_lo_done", "y_done"))
        branch_ms_done, branch_scaled, tap_done, conv_done = (
            sem(n) for n in ("branch_ms_done", "branch_scaled", "tap_done", "conv_done"))
        cos_done, bias_ready, sq_done, sum_done, r_tok_done, branch_r_done, prod_done, act_lo_done = (
            sem(n) for n in ("cos_done", "bias_ready", "sq_done", "sum_done", "r_tok_done", "branch_r_done",
                             "prod_done", "act_lo_done"))
        half_set, zeros_set, mask_begun = sem("half_set"), sem("zeros_set"), sem("mask_begun")
        acc_free = [sem("acc_free0"), sem("acc_free1")]

        def par_col(l, col):
            return par[:, bass.ds(l * NPAR + col, 1)]

        def mix_place(c):
            if c < MIX_ACC:
                return acc[c % 2][:, 0:T]
            return (aux, scores_ps[0], scores_ps[1], pt_ps[0], pt_ps[1], aux)[c - MIX_ACC][:, 0:T]

        block = ctx.enter_context(nc.Block())

        @block.sync
        def _(sp):
            def load(g, s, src, cols):
                sp.wait_ge(split_done, RING * g + s + 1)
                sp.dma_start(w_raw[:, s, 0:cols], src).then_inc(landed[s], 16)

            for i in range(RING):
                c = slice(i * KC // RING, (i + 1) * KC // RING)
                sp.dma_start(x[:, c], xT[:, c]).then_inc(x_landed[i], 16)
                if i == 0:
                    sp.dma_start(par[:], params).then_inc(par_landed, 16)
                load(0, i, w_main[0, i], PIECE)
            sp.dma_start(con[:, O_ID:O_MASK], consts[:, O_ID:O_MASK]).then_inc(id_landed, 16)
            with sp.Fori(0, DEPTH) as l:
                with sp.If(l > 0):
                    for s in range(RING):
                        load(l * GROUPS, s, w_main[bass.ds(l * MAIN, 1), s].rearrange("a p c -> (a p) c"), PIECE)
                with sp.Fori(1, MAIN) as i:
                    for s in range(RING):
                        load(l * GROUPS + i, s, w_main[bass.ds(l * MAIN + i, 1), s].rearrange("a p c -> (a p) c"), PIECE)
                with sp.Fori(0, QUARTERS) as q:
                    with sp.Fori(0, G_UP) as i:
                        for s in range(RING):
                            load(l * GROUPS + q * G_QUARTER + i + G_FFN, s,
                                 w_up[bass.ds(l * FC + q * FQ + i, 1), s].rearrange("a p c -> (a p) c"), PIECE)
                    with sp.Fori(0, G_DOWN) as i:
                        for s in range(RING):
                            load(l * GROUPS + q * G_QUARTER + i + (G_FFN + G_UP), s,
                                 w_down[bass.ds(l * (QUARTERS * G_DOWN) + q * G_DOWN + i, 1), s].rearrange("a p c -> (a p) c"),
                                 PIECE_DOWN)
            for c in range(0, KC, 4):
                sp.wait_ge(y_done, c + 4)
                sp.dma_start(outT[:, c:c + 4], as_chunks[:, c:c + 4]).then_inc(stored, 16)
            sp.wait_ge(stored, 16 * KC // 4)

        @block.tensor
        def _(pe):
            def mm3(out, hi, lo, start, stop, stationary_hi, stationary_lo):
                pe.matmul(out, stationary_hi, hi, start=start, stop=False)
                pe.matmul(out, stationary_hi, lo, start=False, stop=False)
                return pe.matmul(out, stationary_lo, hi, start=False, stop=stop)

            def piece_split(g, s):
                pe.wait_ge(split_done, RING * g + s + (SEED_SLOT + 1))

            def acc_taken(l, rnd, b):
                pe.wait_ge(acc_free[b], l * ROUNDS + rnd + SEED_ACC)

            def chunk(l, g, s0, rnd, b, hi=h_hi, lo=h_lo, before=None):
                acc_taken(l, rnd, b)
                for k in range(KC):
                    s, kk = s0 + k // 8, k % 8
                    if kk == 0:
                        piece_split(g, s)
                    if before:
                        before(k)
                    w = slice(kk * P, (kk + 1) * P)
                    last = mm3(acc[b][:, 0:T], hi[:, k], lo[:, k], k == 0, k == KC - 1, w_hi[s][:, w], w_lo[s][:, w])
                    if kk == 7:
                        last.then_inc(slot_used, 1)

            def two_chunks(l, g, rnd, ks, before=None):
                if ks[0] == 0:
                    acc_taken(l, rnd, 0)
                    acc_taken(l, rnd, 1)
                for k in ks:
                    if before:
                        before(k)
                    for b in range(2):
                        s, kk = 2 * b + k // 8, k % 8
                        if kk == 0:
                            piece_split(g, s)
                        w = slice(kk * P, (kk + 1) * P)
                        out = acc[b][:, 0:T]
                        pe.matmul(out, w_hi[s][:, w], h_hi[:, k], start=k == 0, stop=False)
                        mid = pe.matmul(out, w_hi[s][:, w], h_lo[:, k], start=False, stop=False)
                        last = pe.matmul(out, w_lo[s][:, w], h_hi[:, k], start=False, stop=k == KC - 1)
                        if kk == 7 and b == 0:
                            last.then_inc(slot_used, 1)
                        if k == KC - 1 and b == 1:
                            mid.then_inc(slot_used, 1)
                            last.then_inc(slot_used, 1)

            def norm_sum(n):
                pe.wait_ge(sum_done, n * (KC + 1) + (KC + 1))
                pe.wait_ge(id_landed, 16)
                for t in range(TT):
                    last = pe.matmul(aux[:, T + t:T + t + 1], sq_sum[:, t * P:(t + 1) * P], ones[:, 0:1],
                                     start=True, stop=True)
                last.then_inc(ssq_ready, 1)

            def norm_spread(n):
                for t in range(TT):
                    pe.wait_ge(diag_done, 2 * n + t + 1)
                    last = pe.matmul(aux[:, t * P:(t + 1) * P], ones, diag[:, t], start=True, stop=True)
                last.then_inc(r_ready, 1)

            def rotate(l, i, b):
                pe.wait_ge(acc_free[b], l * ROUNDS + i + (R_PROJ + SEED_ACC + 1))
                pe.wait_ge(rot_read, l * ROT + 2 * i + (b + SEED_ROT_READ))
                pe.matmul(aux[:, 0:T], rot_m, raw[b][:], start=True, stop=True).then_inc(rot_ready, 1)

            def scores(l, pair):
                for hh in range(2):
                    pe.wait_ge(masked, l * (2 * PAIRS) + 2 * pair + (hh - 1 + SEED_HEAD))
                    rows = slice(hh * HD, (hh + 1) * HD)
                    for t in range(TT):
                        last = pe.matmul(scores_ps[hh][:, t * T:(t + 1) * T], q_sb[rows, t * P:(t + 1) * P],
                                         k_sb[rows, :], start=True, stop=True)
                    last.then_inc(scores_ready, 1)

            def transposes(l, pair):
                for hh in range(2):
                    pe.wait_ge(exp_done, l * (2 * PAIRS) + 2 * pair + (hh + 1))
                    pe.wait_ge(pt_ready, l * (2 * PAIRS) + 2 * pair + (hh - 1 + SEED_HEAD))
                    for kb in range(TT):
                        for t in range(TT):
                            last = pe.transpose(pt_ps[hh][:, kb * T + t * P:kb * T + (t + 1) * P],
                                                s_sb[:, hh, t * T + kb * P:t * T + (kb + 1) * P], ident)
                    last.then_inc(transposed, 1)

            def values(l, pair, vcol):
                pe.wait_ge(mixed_done, l * PAIRS + pair + SEED_PAIR)
                for hh in range(2):
                    pe.wait_ge(pt_ready, l * (2 * PAIRS) + 2 * pair + (hh + 1 + SEED_HEAD))
                    for t in range(TT):
                        for kb in range(TT):
                            last = pe.matmul(o_ps[:, (hh * TT + t) * HD:(hh * TT + t + 1) * HD],
                                             pt_sb[:, hh, kb * T + t * P:kb * T + (t + 1) * P],
                                             v[:, kb, bass.ds(vcol + hh * HD, HD)], start=kb == 0, stop=kb == TT - 1)
                last.then_inc(pv_done, 1)


            def mix_t(l, c):
                if c < MIX_ACC:
                    acc_taken(l, R_MIX + c // 2, c % 2)
                if c == MIX_ACC:
                    pe.wait_ge(masked, l * (2 * PAIRS) + (2 * PAIRS + SEED_HEAD))
                for t in range(TT):
                    last = pe.transpose(mix_place(c)[:, t * P:(t + 1) * P], mixed[:, t, c * P:(c + 1) * P], ident)
                last.then_inc(mixt_ready, 1)

            with pe.Fori(0, DEPTH) as l:
                lg = l * GROUPS
                def v_block(blk, first):
                    for half in range(2):
                        for s in range(RING):
                            if first and half == 1 and s == 3:
                                norm_sum(2 * l)
                            piece_split(lg + 2 * blk + half, s)
                            for t in range(TT):
                                if half == 0 and s == 0:
                                    acc_taken(l, blk, t)
                                for kk in range(2):
                                    k = half * 8 + s * 2 + kk
                                    if t == 0 and first:
                                        pe.wait_ge(h_lo_done, l * (2 * KC) + (k + 1))
                                    cols = slice(kk * 512, (kk + 1) * 512)
                                    tok = slice(t * P, (t + 1) * P)
                                    pe.matmul(acc[t][:], h_hi[:, k, tok], w_hi[s][:, cols], start=k == 0, stop=False)
                                    pe.matmul(acc[t][:], h_hi[:, k, tok], w_lo[s][:, cols], start=False, stop=False)
                                    last = pe.matmul(acc[t][:], h_lo[:, k, tok], w_hi[s][:, cols], start=False,
                                                     stop=k == KC - 1)
                                if k == KC - 1 and t == 0:
                                    last.then_inc(v_tile0, 1)
                            last.then_inc(slot_used, 1)

                v_block(0, True)
                norm_spread(2 * l)
                with pe.Fori(1, NVB) as blk:
                    v_block(blk, False)
                pe.wait_ge(con_landed, 16)
                def step_a(i, pairs_before):
                    chunk(l, lg + i + G_PROJ, 0, i + R_PROJ, 0)
                    if pairs_before >= 1:
                        rotate(l, i - 1, 1)
                    if pairs_before >= 2:
                        transposes(l, i - 2)
                    chunk(l, lg + i + G_PROJ, 2, i + R_PROJ, 1)
                    if pairs_before >= 2:
                        values(l, i - 2, (i - 2) * P)
                    if pairs_before >= 1:
                        pe.wait_ge(rot_done, l * ROT + 2 * i + SEED_ROT)
                        scores(l, i - 1)
                    rotate(l, i, 0)

                step_a(0, 0)
                step_a(1, 1)
                with pe.Fori(2, PA) as i:
                    step_a(i, 2)

                chunk(l, lg + G_PROJ + PA, 0, R_PROJ + PA, 0)
                rotate(l, PA - 1, 1)
                transposes(l, PA - 2)
                chunk(l, lg + G_PROJ + PA, 2, R_PROJ + PA, 1)
                values(l, PA - 2, (PA - 2) * P)
                pe.wait_ge(rot_done, l * ROT + 2 * PA + SEED_ROT)
                scores(l, PA - 1)
                rotate(l, PA, 0)
                rotate(l, PA, 1)
                for j in range(1, PB):
                    r = 2 * PA + 1 + j
                    pair = PA + j
                    chunk(l, lg + G_PROJ + r // 2, 2 * (r % 2), R_PROJ + r // 2, r % 2)
                    transposes(l, pair - 2)
                    pe.wait_ge(rot_done, l * ROT + r + SEED_ROT)
                    scores(l, pair - 1)
                    rotate(l, r // 2, r % 2)
                    values(l, pair - 2, (PA - 1) * P if j == 1 else WA)

                def step_c(i):
                    pair, at = PA + PB + i, PA + 3 + i
                    chunk(l, lg + G_PROJ + at, 0, R_PROJ + at, 0)
                    transposes(l, pair - 2)
                    if i == 0:
                        pe.wait_ge(rot_done, l * ROT + ROT + SEED_ROT)
                    else:
                        pe.wait_ge(acc_free[0], l * ROUNDS + (R_PROJ + at + SEED_ACC))
                        pe.wait_ge(acc_free[1], l * ROUNDS + (R_PROJ + at + SEED_ACC))
                    scores(l, pair - 1)
                    chunk(l, lg + G_PROJ + at, 2, R_PROJ + at, 1)
                    values(l, pair - 2, WA if i < 2 else WA + WKV + (i - 2) * P)

                for i in range(PC):
                    step_c(i)

                def mix_ready(k):
                    if k < MIX_ACC:
                        pe.wait_ge(acc_free[k % 2], l * ROUNDS + (R_MIX + k // 2 + SEED_ACC + 1))
                    else:
                        pe.wait_ge(mix_lo_done, l * (KC - MIX_ACC) + (k - MIX_ACC + 1))

                transposes(l, PAIRS - 2)
                acc_taken(l, R_MIX, 0)
                acc_taken(l, R_MIX, 1)
                scores(l, PAIRS - 1)
                values(l, PAIRS - 2, WA + WKV + (PC - 2) * P)
                pe.wait_ge(branch_scaled, 3 * l + 1)
                for c in range(PA):
                    mix_t(l, c)
                pe.wait_ge(branch_scaled, 3 * l + 2)
                for c in range(PA, PA + PB):
                    mix_t(l, c)
                two_chunks(l, lg + G_OUT, R_OUT, range(0, 5), mix_ready)
                transposes(l, PAIRS - 1)
                two_chunks(l, lg + G_OUT, R_OUT, range(5, 9), mix_ready)
                values(l, PAIRS - 1, WA + WKV + (PC - 1) * P)
                two_chunks(l, lg + G_OUT, R_OUT, range(9, PA + PB), mix_ready)
                pe.wait_ge(branch_scaled, 3 * l + 3)
                for c in range(PA + PB, KC):
                    mix_t(l, c)
                two_chunks(l, lg + G_OUT, R_OUT, range(PA + PB, KC), mix_ready)

                with pe.Fori(1, KC // 2) as i:
                    chunk(l, lg + i + G_OUT, 0, i + R_OUT, 0)
                    chunk(l, lg + i + G_OUT, 2, i + R_OUT, 1)

                def h2_ready(k):
                    pe.wait_ge(h_lo_done, l * (2 * KC) + (KC + k + 1))
                    if k == 8:
                        norm_sum(2 * l + 1)

                def spread(k):
                    if k == 0:
                        norm_spread(2 * l + 1)

                def quarter(q, first):
                    g0, r0 = lg + q * G_QUARTER, q * R_QUARTER
                    chunk(l, g0 + G_FFN, 0, r0 + R_FFN, 0, h2_hi, h2_lo, h2_ready if first else None)
                    chunk(l, g0 + G_FFN, 2, r0 + R_FFN, 1, h2_hi, h2_lo, spread if first else None)
                    with pe.Fori(1, FQ) as j:
                        chunk(l, g0 + j + G_FFN, 0, r0 + j + R_FFN, 0, h2_hi, h2_lo)
                        chunk(l, g0 + j + G_FFN, 2, r0 + j + R_FFN, 1, h2_hi, h2_lo)

                    def down_products(s, ks):
                        for k in ks:
                            w = slice(k * P, (k + 1) * P)
                            last = mm3(acc[s % 2][:, 0:T], act_hi[:, k], act_lo[:, k], k == 0, k == FQ - 1,
                                       w_hi[s][:, w], w_lo[s][:, w])
                        return last

                    def down_begin(i, s):
                        acc_taken(l, r0 + 2 * i + (R_FFN + FQ + s // 2), s % 2)
                        piece_split(g0 + i + (G_FFN + G_UP), s)

                    for s in range(2):
                        down_begin(0, s)
                        if s == 0:
                            pe.wait_ge(act_lo_done, l * FC + q * FQ + (FQ - 1 + SEED_PROD))
                        down_products(s, range(FQ - 1))
                    pe.wait_ge(act_lo_done, l * FC + q * FQ + (FQ + SEED_PROD))
                    for s in range(2):
                        down_products(s, [FQ - 1]).then_inc(slot_used, 1)
                    for s in range(2, RING):
                        down_begin(0, s)
                        down_products(s, range(FQ)).then_inc(slot_used, 1)
                    with pe.Fori(1, G_DOWN) as i:
                        for s in range(RING):
                            down_begin(i, s)
                            down_products(s, range(FQ)).then_inc(slot_used, 1)

                quarter(0, True)
                with pe.Fori(1, QUARTERS) as q:
                    quarter(q, False)
            norm_sum(2 * DEPTH)
            norm_spread(2 * DEPTH)

        @block.scalar
        def _(act):
            def hi(g, s, cols=PIECE):
                act.wait_ge(landed[s], 16 * g + 16)
                act.wait_ge(slot_used, RING * g + s + 1)
                act.activation(w_hi[s][:, 0:cols], w_raw[:, s, 0:cols], ACT.Copy).then_inc(hi_done, 1)

            def chunk_ready(g, s):
                act.wait_ge(slot_used, RING * g + s + (SEED_SLOT + 1))

            def h_chunk_hi(c, to, gain):
                act.activation(to[:, bass.ds(c, 1)].rearrange("p a t -> p (a t)"),
                               x[:, bass.ds(c, 1)].rearrange("p a t -> p (a t)"), ACT.Copy,
                               scale=gain).then_inc(h_hi_done, 1)

            def copy_pt(l, pair):
                for hh in range(2):
                    act.wait_ge(transposed, l * (2 * PAIRS) + 2 * pair + (hh + 1 + SEED_HEAD))
                    act.wait_ge(pv_done, l * PAIRS + pair + SEED_PAIR)
                    act.activation(pt_sb[:, hh], pt_ps[hh][:], ACT.Copy).then_inc(pt_ready, 1)

            def exps(l, pair, sink=None):
                act.wait_ge(recip_done, l * PAIRS + pair + SEED_PAIR)
                for hh in range(2):
                    act.wait_ge(maxed, l * (2 * PAIRS) + 2 * pair + (hh + 1))
                    if sink is not None:
                        act.activation(esink[:, 2 * hh:2 * hh + 2], nmx[:, 2 * hh:2 * hh + 2], ACT.Exp,
                                       bias=par_col(l, O_SINK + 2 * sink + hh))
                    for t in range(TT):
                        at = slice(t * T, (t + 1) * T)
                        last = act.activation(s_sb[:, hh, at], s_sb[:, hh, at], ACT.Exp,
                                              bias=nmx[:, 2 * hh + t:2 * hh + t + 1],
                                              accum_out=den[:, 2 * hh + t:2 * hh + t + 1])
                    last.then_inc(exp_done, 1)

            def branch_squares(l, part):
                first, end = (0, PA, PA + PB, PAIRS - 1, PAIRS)[part:part + 2]
                act.wait_ge(mixed_done, l * PAIRS + (end + SEED_PAIR))
                for t in range(TT):
                    act.wait_ge(branch_sq, 4 * TT * l + (TT * part + t + SEED_SQ))
                    act.activation(junk[:, 0:(end - first) * P], mixed[:, t, first * P:end * P], ACT.Square,
                                   accum_out=branch_ssq[:, part, t:t + 1]).then_inc(branch_sq, 1)

            def mix_hi(l, c):
                act.wait_ge(mixt_ready, l * KC + (c + 1))
                act.activation(h_hi[:, c], mix_place(c), ACT.Copy,
                               scale=par_col(l, O_MIX + c)).then_inc(mix_hi_done, 1)

            act.wait_ge(half_set, 1)
            act.activation(silu_first[:], minus_half[:], ACT.Copy)
            act.wait_ge(par_landed, 16)
            for i in range(RING):
                act.wait_ge(x_landed[i], 16)
                for c in range(i * KC // RING, (i + 1) * KC // RING):
                    h_chunk_hi(c, h_hi, par[:, O_LN1 + c:O_LN1 + c + 1])
                hi(0, i)
            with act.Fori(0, DEPTH) as l:
                lg = l * GROUPS
                with act.Fori(0, NVB) as blk:
                    for s in range(RING):
                        hi(lg + 2 * blk + 1, s)
                    for s in range(RING - 1):
                        hi(lg + 2 * blk + 2, s)
                    act.wait_ge(r_tok_done, 2 * l + 1)
                    act.wait_ge(v_tile0, NVB * l + blk + 1)
                    act.activation(v[:, 0, bass.ds(blk * 512, 512)], acc[0][:], ACT.Copy,
                                   scale=r_tok[:, 0:1]).then_inc(acc_free[0], 1)
                    hi(lg + 2 * blk + 2, RING - 1)
                    act.activation(v[:, 1, bass.ds(blk * 512, 512)], acc[1][:], ACT.Copy,
                                   scale=r_tok[:, 1:2]).then_inc(acc_free[1], 1)

                def step_a(i, pairs_before):
                    g = lg + i + (G_PROJ + 1)
                    hi(g, 0)
                    hi(g, 1)
                    if pairs_before >= 2:
                        copy_pt(l, i - 2)
                    hi(g, 2)
                    hi(g, 3)
                    if pairs_before >= 1:
                        exps(l, i - 1)

                step_a(0, 0)
                step_a(1, 1)
                with act.Fori(2, PA) as i:
                    step_a(i, 2)
                g = lg + (G_PROJ + PA + 1)
                hi(g, 0)
                hi(g, 1)
                copy_pt(l, PA - 2)
                hi(g, 2)
                hi(g, 3)
                exps(l, PA - 1)
                for j in range(1, PB):
                    r = 2 * PA + 1 + j
                    g = lg + (G_PROJ + r // 2 + 1)
                    hi(g, 2 * (r % 2))
                    hi(g, 2 * (r % 2) + 1)
                    copy_pt(l, PA + j - 2)
                    exps(l, PA + j - 1, sink=j - 1)
                for i in range(PC):
                    g = lg + (G_PROJ + PA + 3 + i + 1)
                    pair = PA + PB + i
                    hi(g, 0)
                    hi(g, 1)
                    copy_pt(l, pair - 2)
                    hi(g, 2)
                    exps(l, pair - 1, sink=PB - 1 if i == 0 else None)
                    hi(g, 3)
                    if i == 1:
                        branch_squares(l, 0)
                    if i == 3:
                        branch_squares(l, 1)
                copy_pt(l, PAIRS - 2)
                exps(l, PAIRS - 1)
                for c in range(PA):
                    mix_hi(l, c)
                branch_squares(l, 2)
                for c in range(PA, PA + PB):
                    mix_hi(l, c)
                copy_pt(l, PAIRS - 1)
                branch_squares(l, 3)
                for c in range(PA + PB, KC):
                    mix_hi(l, c)
                act.activation(silu_first[:], minus_half[:], ACT.Silu)
                with act.Fori(0, KC // 2) as i:
                    for b in range(2):
                        hi(lg + i + (G_OUT + 1), 2 * b)
                        hi(lg + i + (G_OUT + 1), 2 * b + 1)
                        act.wait_ge(acc_free[b], l * ROUNDS + i + (R_OUT + SEED_ACC + 1))
                        h_chunk_hi(2 * i + b, h2_hi, par[:, bass.ds(l * NPAR + 2 * i + (O_LN2 + b), 1)])

                def quarter(q, last):
                    g0 = lg + q * G_QUARTER

                    def product_hi(j):
                        act.wait_ge(prod_done, l * FC + q * FQ + j + (SEED_PROD + 1))
                        act.activation(act_hi[:, bass.ds(j, 1)].rearrange("p a t -> p (a t)"), prod[:],
                                       ACT.Copy).then_inc(act_hi_done, 1)

                    def up(j, cols, first=False):
                        g = g0 + j + (G_FFN + 1)
                        f = q * FQ + j
                        col = l * NPAR + 8 * f
                        hi(g, 0, cols)
                        if not first:
                            product_hi(j - 1)
                        hi(g, 1, cols)
                        act.wait_ge(acc_free[0], l * ROUNDS + q * R_QUARTER + j + (R_FFN + SEED_ACC + 1))
                        act.activation(gate[:], z[0][:], ACT.Identity,
                                       scale=par[:, bass.ds(col + (O_CONV + 1), 1)],
                                       bias=par[:, bass.ds(col + (O_CONV + 3), 1)]).then_inc(affine_done, 1)
                        hi(g, 2, cols)
                        act.wait_ge(conv_done, l * (2 * FC) + 2 * f + (1 + SEED_CONV))
                        act.wait_ge(prod_done, l * FC + f + SEED_PROD)
                        act.activation(silu[:], gate[:], ACT.Silu).then_inc(silu_done, 1)
                        hi(g, 3, cols)
                        act.wait_ge(acc_free[1], l * ROUNDS + q * R_QUARTER + j + (R_FFN + SEED_ACC + 1))
                        act.activation(value[:], z[1][:], ACT.Identity,
                                       scale=par[:, bass.ds(col + (O_CONV + 5), 1)],
                                       bias=par[:, bass.ds(col + (O_CONV + 7), 1)]).then_inc(affine_done, 1)

                    up(0, PIECE, True)
                    with act.Fori(1, FQ - 1) as j:
                        up(j, PIECE)
                    up(FQ - 1, PIECE_DOWN)
                    product_hi(FQ - 1)

                    def down(i, s):
                        if last:
                            act.wait_ge(acc_free[s % 2], l * ROUNDS + 2 * i
                                        + (QUARTERS * R_QUARTER - R_QUARTER + R_FFN + FQ + s // 2 + SEED_ACC + 1))
                            h_chunk_hi(4 * i + s, h_hi, par[:, bass.ds(l * NPAR + 4 * i + (NPAR + O_LN1 + s), 1)])

                    with act.Fori(0, G_DOWN - 1) as i:
                        for s in range(RING):
                            hi(g0 + i + (G_FFN + G_UP + 1), s, PIECE_DOWN)
                            down(i, s)
                    if last:
                        for s in range(RING):
                            down(G_DOWN - 1, s)
                            with act.If(l < DEPTH - 1):
                                hi(g0 + (G_FFN + G_QUARTER), s)
                    else:
                        for s in range(RING):
                            hi(g0 + (G_FFN + G_QUARTER), s)

                with act.Fori(0, QUARTERS - 1) as q:
                    quarter(q, False)
                quarter(QUARTERS - 1, True)

        @block.vector
        def _(dve):
            def lo(g, s, cols=PIECE):
                dve.wait_ge(hi_done, RING * g + s + 1)
                dve.tensor_tensor(w_lo[s][:, 0:cols], w_raw[:, s, 0:cols], w_hi[s][:, 0:cols].bitcast(F32),
                                  ALU.subtract).then_inc(split_done, 1)

            def norm_mean(n):
                dve.wait_ge(ssq_ready, n + 1)
                dve.tensor_scalar(ms[:], aux[:, T:T + TT], 1.0 / D, EPS, ALU.mult, ALU.add).then_inc(ms_done, 1)

            def norm_diag(n):
                dve.wait_ge(r_tok_done, n + 1)
                for t in range(TT):
                    dve.tensor_scalar(diag[:, t], ident, r_tok[:, t:t + 1], None, ALU.mult).then_inc(diag_done, 1)

            def norm_end(n):
                dve.wait_ge(r_ready, n + 1)
                dve.tensor_copy(r_all[:], aux[:, 0:T]).then_inc(r_all_done, 1)

            def h_chunk_lo(n, c, hi, lo, gain):
                dve.wait_ge(h_hi_done, n * KC + c + 1)
                at = bass.ds(c, 1)
                dve.scalar_tensor_tensor(lo[:, at].rearrange("p a t -> p (a t)"), x[:, at].rearrange("p a t -> p (a t)"),
                                         gain, hi[:, at].rearrange("p a t -> p (a t)").bitcast(F32),
                                         ALU.mult, ALU.subtract).then_inc(h_lo_done, 1)

            def take(l, i, b, to, is_q):
                dve.wait_ge(slot_used, RING * (l * GROUPS + i + G_PROJ) + (1 + 2 * b + SEED_SLOT + 1))
                dve.scalar_tensor_tensor(to[:], acc[b][:, 0:T], HD ** -0.5 if is_q else 1.0, r_all[:],
                                         ALU.mult, ALU.mult).then_inc(acc_free[b], 1)

            def take_raw(l, i, b, is_q):
                dve.wait_ge(rot_done, l * ROT + 2 * i + (b - 1 + SEED_ROT))
                take(l, i, b, raw[b], is_q)

            def take_c(l, i, b):
                dve.wait_ge(scores_ready, l * (2 * PAIRS) + 2 * (PA + PB + i) + SEED_SCORES)
                take(l, PA + 3 + i, b, (q_sb, k_sb)[b], b == 0)

            def rotated(l, i, b, pair, is_q):
                dve.wait_ge(rot_ready, l * ROT + 2 * i + (b + 1))
                dve.wait_ge(rot_done, l * ROT + 2 * i + (b + SEED_ROT))
                dve.tensor_tensor(rot_sin[:], aux[:, 0:T], sin, ALU.mult).then_inc(rot_read, 1)
                dve.wait_ge(rot_read, l * ROT + 2 * i + (b + SEED_ROT_READ + 1))
                dve.wait_ge(cos_done, l * ROT + 2 * i + (b + 1))
                dve.wait_ge(scores_ready, l * (2 * PAIRS) + 2 * pair + SEED_SCORES)
                dve.tensor_tensor((q_sb if is_q else k_sb)[:], rot_sin[:], rot_cos[:], ALU.add).then_inc(rot_done, 1)

            def mask(l, pair, masks, sink=None):
                for hh in range(2):
                    dve.wait_ge(scores_ready, l * (2 * PAIRS) + 2 * pair + (hh + 1 + SEED_SCORES))
                    dve.wait_ge(transposed, l * (2 * PAIRS) + 2 * pair + (hh - 1 + SEED_HEAD))
                    dve.sem_inc(mask_begun, 1)
                    for t in range(TT):
                        at = slice(t * T, (t + 1) * T)
                        last = dve.tensor_tensor_reduce(s_sb[:, hh, at], scores_ps[hh][:, at], masks[hh][:, at], 1.0,
                                                        -3e38, ALU.add, ALU.max, mx[:, 2 * hh + t:2 * hh + t + 1])
                    last.then_inc(masked, 1)
                    dve.wait_ge(masked, l * (2 * PAIRS) + 2 * pair + (hh + 1 + SEED_HEAD))
                    if sink is None:
                        last = dve.tensor_scalar(nmx[:, 2 * hh:2 * hh + 2], mx[:, 2 * hh:2 * hh + 2], -1.0, None, ALU.mult)
                    else:
                        last = dve.tensor_scalar(nmx[:, 2 * hh:2 * hh + 2], mx[:, 2 * hh:2 * hh + 2],
                                                 par_col(l, O_SINK + 2 * sink + hh), -1.0, ALU.max, ALU.mult)
                    last.then_inc(maxed, 1)

            def recip(l, pair, sink=None):
                dve.wait_ge(exp_done, l * (2 * PAIRS) + 2 * pair + 2)
                total = den
                if sink is not None:
                    dve.tensor_tensor(den_all[:], den[:], esink[:], ALU.add).then_inc(den_done, 1)
                    dve.wait_ge(den_done, PB * l + (sink + 1))
                    total = den_all
                dve.wait_ge(mixed_done, l * PAIRS + pair + SEED_PAIR)
                dve.reciprocal(rden[:], total[:]).then_inc(recip_done, 1)

            def outputs(l, pair):
                dve.wait_ge(recip_done, l * PAIRS + pair + (1 + SEED_PAIR))
                dve.wait_ge(pv_done, l * PAIRS + pair + (1 + SEED_PAIR))
                to = mixed[:, :, bass.ds(pair * P, P)].rearrange("p t (h d) -> p h t d", h=2)
                dve.tensor_tensor(to, o_ps[:, 0:2 * TT * HD].rearrange("p (h t d) -> p h t d", h=2, t=TT),
                                  rden[:].rearrange("p (h t) -> p h t", h=2).unsqueeze(3).to_broadcast([P, 2, TT, HD]),
                                  ALU.mult).then_inc(mixed_done, 1)

            def branch_norm(l, br):
                o, w = BRANCHES[br]
                parts = TT * (br + 1) if br < 2 else 4 * TT
                dve.wait_ge(branch_sq, 4 * TT * l + (parts + SEED_SQ))
                if br < 2:
                    last = dve.tensor_scalar(branch_ms[:, br], branch_ssq[:, br], w * EPS, None, ALU.add)
                else:
                    last = dve.scalar_tensor_tensor(branch_ms[:, br], branch_ssq[:, 2], w * EPS, branch_ssq[:, 3],
                                                    ALU.add, ALU.add)
                last.then_inc(branch_ms_done, 1)
                dve.wait_ge(branch_r_done, 3 * l + (br + 1))
                for t in range(TT):
                    last = dve.tensor_scalar(mixed[:, t, o:o + w], mixed[:, t, o:o + w], branch_r[:, br, t:t + 1],
                                             float(w) ** 0.5, ALU.mult, ALU.mult)
                last.then_inc(branch_scaled, 1)

            def mix_lo(l, c):
                dve.wait_ge(mix_hi_done, l * KC + (c + 1))
                last = dve.scalar_tensor_tensor(h_lo[:, c], mix_place(c), par_col(l, O_MIX + c), h_hi[:, c].bitcast(F32),
                                                ALU.mult, ALU.subtract)
                last.then_inc(acc_free[c % 2] if c < MIX_ACC else mix_lo_done, 1)

            def add_to_x(g, s, m, b, squared):
                dve.wait_ge(slot_used, RING * g + s + (SEED_SLOT + 1))
                dve.wait_ge(sq_done, squared)
                xm = x[:, bass.ds(m, 1)].rearrange("p a t -> p (a t)")
                dve.tensor_tensor(xm, acc[b][:, 0:T], xm, ALU.add).then_inc(acc_free[b], 1)

            for s_, n in ((slot_used, SEED_SLOT), (split_done, SEED_SLOT), (acc_free[0], SEED_ACC),
                          (acc_free[1], SEED_ACC), (scores_ready, SEED_SCORES), (transposed, SEED_HEAD),
                          (masked, SEED_HEAD), (pt_ready, SEED_HEAD), (pv_done, SEED_PAIR), (recip_done, SEED_PAIR),
                          (mixed_done, SEED_PAIR), (rot_done, SEED_ROT), (rot_read, SEED_ROT_READ),
                          (conv_done, SEED_CONV), (prod_done, SEED_PROD), (act_lo_done, SEED_PROD), (branch_sq, SEED_SQ)):
                dve.sem_inc(s_, n)
            dve.wait_ge(par_landed, 16)
            for i in range(RING):
                dve.wait_ge(x_landed[i], 16)
                for c in range(i * KC // RING, (i + 1) * KC // RING):
                    h_chunk_lo(0, c, h_hi, h_lo, par[:, O_LN1 + c:O_LN1 + c + 1])
                lo(0, i)
            dve.wait_ge(id_landed, 16)
            with dve.Fori(0, DEPTH) as l:
                lg = l * GROUPS
                for s in range(RING):
                    lo(lg + 1, s)
                lo(lg + 2, 0)
                lo(lg + 2, 1)
                norm_mean(2 * l)
                lo(lg + 2, 2)
                norm_diag(2 * l)
                lo(lg + 2, 3)
                norm_end(2 * l)
                with dve.Fori(2, 2 * NVB) as i:
                    for s in range(RING):
                        lo(lg + i + 1, s)

                dve.wait_ge(r_all_done, 2 * l + 1)
                dve.wait_ge(con_landed, 16)
                dve.wait_ge(mask_landed, 16)
                masks_a, masks_b = (mask_a, mask_a), (mask_b, mask_b)

                def step_a(i, pairs_before):
                    g = lg + i + (G_PROJ + 1)
                    lo(g, 0)
                    if pairs_before >= 2:
                        recip(l, i - 2)
                    if pairs_before >= 1:
                        rotated(l, i - 1, 1, i - 1, False)
                    take_raw(l, i, 0, True)
                    lo(g, 1)
                    lo(g, 2)
                    take_raw(l, i, 1, False)
                    lo(g, 3)
                    if pairs_before >= 2:
                        outputs(l, i - 2)
                    if pairs_before >= 1:
                        mask(l, i - 1, masks_a)
                    rotated(l, i, 0, i, True)

                step_a(0, 0)
                step_a(1, 1)
                with dve.Fori(2, PA) as i:
                    step_a(i, 2)
                g = lg + (G_PROJ + PA + 1)
                lo(g, 0)
                recip(l, PA - 2)
                rotated(l, PA - 1, 1, PA - 1, False)
                take_raw(l, PA, 0, False)
                lo(g, 1)
                lo(g, 2)
                take_raw(l, PA, 1, True)
                lo(g, 3)
                outputs(l, PA - 2)
                mask(l, PA - 1, masks_a)
                rotated(l, PA, 0, PA, False)
                rotated(l, PA, 1, PA, True)
                for j in range(1, PB):
                    r = 2 * PA + 1 + j
                    g = lg + (G_PROJ + r // 2 + 1)
                    lo(g, 2 * (r % 2))
                    take_raw(l, r // 2, r % 2, True)
                    lo(g, 2 * (r % 2) + 1)
                    recip(l, PA + j - 2, sink=j - 2 if j >= 2 else None)
                    mask(l, PA + j - 1, masks_b, sink=j - 1)
                    rotated(l, r // 2, r % 2, PA + j, True)
                    outputs(l, PA + j - 2)
                for i in range(PC):
                    g = lg + (G_PROJ + PA + 3 + i + 1)
                    pair = PA + PB + i
                    if i == 1:
                        dve.wait_ge(bias_ready, HC * (l + 1))
                    recip(l, pair - 2, sink=PB - 2 + i if i < 2 else None)
                    lo(g, 0)
                    lo(g, 1)
                    if i == 0:
                        mask(l, pair - 1, masks_b, sink=PB - 1)
                    else:
                        mask(l, pair - 1, (bias[:, 2 * i - 2], bias[:, 2 * i - 1]))
                    take_c(l, i, 0)
                    lo(g, 2)
                    lo(g, 3)
                    take_c(l, i, 1)
                    outputs(l, pair - 2)
                    if i == 2:
                        branch_norm(l, 0)
                    if i == 4:
                        branch_norm(l, 1)
                recip(l, PAIRS - 2)
                mask(l, PAIRS - 1, (bias[:, HC - 2], bias[:, HC - 1]))
                outputs(l, PAIRS - 2)
                for c in range(PA + PB):
                    mix_lo(l, c)
                recip(l, PAIRS - 1)
                outputs(l, PAIRS - 1)
                branch_norm(l, 2)
                for c in range(PA + PB, KC):
                    mix_lo(l, c)

                with dve.Fori(0, KC // 2) as i:
                    g = lg + i + G_OUT
                    for b in range(2):
                        lo(g + 1, 2 * b)
                        add_to_x(g, 1 + 2 * b, 2 * i + b, b, l * (2 * KC) + 2 * i + (b + 1))
                        lo(g + 1, 2 * b + 1)
                        h_chunk_lo(2 * l + 1, 2 * i + b, h2_hi, h2_lo,
                                   par[:, bass.ds(l * NPAR + 2 * i + (O_LN2 + b), 1)])

                def quarter(q, first, last):
                    g0 = lg + q * G_QUARTER

                    def up(j, cols):
                        g = g0 + j + (G_FFN + 1)
                        f = q * FQ + j
                        col = l * NPAR + 8 * f
                        for b, u in ((0, gate), (1, value)):
                            lo(g, 2 * b, cols)
                            dve.wait_ge(r_all_done, 2 * l + 2)
                            dve.wait_ge(slot_used, RING * (g - 1) + (1 + 2 * b + SEED_SLOT + 1))
                            dve.wait_ge(conv_done, l * (2 * FC) + 2 * f + (b - 1 + SEED_CONV))
                            dve.tensor_tensor(z[b][:], acc[b][:, 0:T], r_all[:], ALU.mult).then_inc(acc_free[b], 1)
                            lo(g, 2 * b + 1, cols)
                            dve.wait_ge(affine_done, l * (2 * FC) + 2 * f + (b + 1))
                            dve.scalar_tensor_tensor(u[:, 1:T], z[b][:, 0:T - 1],
                                                     par[:, bass.ds(col + (O_CONV + 4 * b), 1)], u[:, 1:T],
                                                     ALU.mult, ALU.add).then_inc(tap_done, 1)
                            dve.wait_ge(tap_done, l * (2 * FC) + 2 * f + (b + 1))
                            dve.scalar_tensor_tensor(u[:, 0:T - 1], z[b][:, 1:T],
                                                     par[:, bass.ds(col + (O_CONV + 4 * b + 2), 1)], u[:, 0:T - 1],
                                                     ALU.mult, ALU.add).then_inc(conv_done, 1)

                    if first:
                        norm_mean(2 * l + 1)
                        norm_diag(2 * l + 1)
                        norm_end(2 * l + 1)
                    with dve.Fori(0, FQ - 1) as j:
                        up(j, PIECE)
                    up(FQ - 1, PIECE_DOWN)

                    def down_add(i, s):
                        add_to_x(g0 + i + (G_FFN + G_UP), s, 4 * i + s, s % 2, l * (2 * KC) + 4 * i + (KC + s + 1))

                    def down_lo(i, s):
                        if last:
                            h_chunk_lo(2 * l + 2, 4 * i + s, h_hi, h_lo,
                                       par[:, bass.ds(l * NPAR + 4 * i + (NPAR + O_LN1 + s), 1)])

                    with dve.Fori(0, G_DOWN - 1) as i:
                        for s in range(RING):
                            down_add(i, s)
                            lo(g0 + i + (G_FFN + G_UP + 1), s, PIECE_DOWN)
                            down_lo(i, s)
                    for s in range(RING):
                        down_add(G_DOWN - 1, s)
                        down_lo(G_DOWN - 1, s)
                        if not last:
                            lo(g0 + (G_FFN + G_QUARTER), s)
                        else:
                            with dve.If(l < DEPTH - 1):
                                lo(g0 + (G_FFN + G_QUARTER), s)

                quarter(0, True, False)
                with dve.Fori(1, QUARTERS - 1) as q:
                    quarter(q, False, False)
                quarter(QUARTERS - 1, False, True)
            norm_mean(2 * DEPTH)
            norm_diag(2 * DEPTH)
            norm_end(2 * DEPTH)
            dve.wait_ge(r_all_done, 2 * DEPTH + 1)
            for c in range(KC):
                dve.scalar_tensor_tensor(as_chunks[:, c], x[:, c], par[:, DEPTH * NPAR + c:DEPTH * NPAR + c + 1], r_all[:],
                                         ALU.mult, ALU.mult).then_inc(y_done, 1)

        @block.gpsimd
        def _(pool):
            pool.memset(minus_half[:], -0.5).then_inc(half_set, 1)
            pool.memset(zeros[:], 0.0).then_inc(zeros_set, 1)
            pool.wait_ge(zeros_set, 1)

            def squares_begin():
                pool.tensor_tensor(sq_sum[:], zeros[:], zeros[:], ALU.add).then_inc(sum_done, 1)

            def square(n, c):
                xc = x[:, bass.ds(c, 1)].rearrange("p a t -> p (a t)")
                pool.wait_ge(sum_done, n * (KC + 1) + c + 1)
                pool.tensor_tensor(sq[:], xc, xc, ALU.mult).then_inc(sq_done, 1)
                pool.wait_ge(sq_done, n * KC + c + 1)
                pool.tensor_tensor(sq_sum[:], sq_sum[:], sq[:], ALU.add).then_inc(sum_done, 1)

            def norm(n):
                pool.wait_ge(ms_done, n + 1)
                pool.tensor_tensor(r_tok[:], ms[:], minus_half[:], ALU.pow).then_inc(r_tok_done, 1)

            def cos_product(l, i, b):
                pool.wait_ge(acc_free[b], l * ROUNDS + i + (R_PROJ + SEED_ACC + 1))
                pool.wait_ge(rot_done, l * ROT + 2 * i + (b + SEED_ROT))
                pool.tensor_tensor(rot_cos[:], raw[b][:], cos, ALU.mult).then_inc(cos_done, 1)

            def branch_rsqrt(l, br):
                pool.wait_ge(branch_ms_done, 3 * l + (br + 1))
                pool.tensor_tensor(branch_r[:, br], branch_ms[:, br], minus_half[:], ALU.pow).then_inc(branch_r_done, 1)

            squares_begin()
            for i in range(RING):
                pool.wait_ge(x_landed[i], 16)
                for c in range(i * KC // RING, (i + 1) * KC // RING):
                    square(0, c)
            pool.wait_ge(half_set, 1)
            pool.dma_start(con[:, 0:O_ID], consts[:, 0:O_ID]).then_inc(con_landed, 16)
            pool.dma_start(con[:, O_MASK:NCONST], consts[:, O_MASK:NCONST]).then_inc(mask_landed, 16)
            with pool.Fori(0, DEPTH) as l:
                pool.dma_start(bias[:], bias_c[bass.ds(l, 1)].rearrange("a p h c -> (a p) h c")).then_inc(bias_landed, 16)
                norm(2 * l)
                pool.wait_ge(con_landed, 16)
                pool.wait_ge(mask_landed, 16)
                pool.wait_ge(bias_landed, 16 * l + 16)
                for hc in range(HC):
                    pool.tensor_tensor(bias[:, hc], bias[:, hc], mask_c, ALU.add).then_inc(bias_ready, 1)
                with pool.Fori(0, ROT // 2) as i:
                    cos_product(l, i, 0)
                    cos_product(l, i, 1)
                for br in range(3):
                    branch_rsqrt(l, br)
                pool.wait_ge(ssq_ready, 2 * l + 1)
                squares_begin()
                with pool.Fori(0, KC // 2) as i:
                    for b in range(2):
                        pool.wait_ge(acc_free[b], l * ROUNDS + i + (R_OUT + SEED_ACC + 1))
                        square(2 * l + 1, 2 * i + b)
                norm(2 * l + 1)
                with pool.Fori(0, QUARTERS) as q:
                    with pool.Fori(0, FQ) as j:
                        f = q * FQ + j
                        pool.wait_ge(silu_done, l * FC + f + 1)
                        pool.wait_ge(conv_done, l * (2 * FC) + 2 * f + (2 + SEED_CONV))
                        pool.wait_ge(act_lo_done, l * FC + f + SEED_PROD)
                        pool.tensor_tensor(prod[:], silu[:], value[:], ALU.mult).then_inc(prod_done, 1)
                        pool.wait_ge(act_hi_done, l * FC + f + 1)
                        at = bass.ds(j, 1)
                        pool.tensor_tensor(act_lo[:, at].rearrange("p a t -> p (a t)"), prod[:],
                                           act_hi[:, at].rearrange("p a t -> p (a t)").bitcast(F32),
                                           ALU.subtract).then_inc(act_lo_done, 1)
                pool.wait_ge(sum_done, (2 * l + 2) * (KC + 1))
                pool.wait_ge(ssq_ready, 2 * l + 2)
                squares_begin()
                with pool.Fori(0, KC // 2) as i:
                    for b in range(2):
                        pool.wait_ge(acc_free[b], l * ROUNDS + i
                                     + (QUARTERS * R_QUARTER - R_QUARTER + R_FFN + FQ + SEED_ACC + 1))
                        square(2 * l + 2, 2 * i + b)
            norm(2 * DEPTH)


def _constants():
    f32 = np.float32
    inv = (f32(10000.0) ** (-np.arange(0, HD, 2, dtype=f32) / f32(HD))).astype(f32)
    ang = np.arange(T, dtype=f32)[:, None] * inv[None, :]
    four = np.tile(ang.T, (4, 1))
    swap = np.zeros((P, P), f32)
    half = HD // 2
    for base in (0, HD):
        for d in range(half):
            swap[base + half + d, base + d] = -1.0
            swap[base + d, base + half + d] = 1.0
    q, k = np.arange(T)[:, None], np.arange(T)[None, :]
    times = np.zeros((T, T))
    for window, r in ((128, 1), (512, 4), (2048, 16)):
        times += (q % r == k % r) & (np.abs(q // r - k // r) <= window // (2 * r))
    m_a = np.where(times > 0, np.log(np.maximum(times, 1.0)), NEG)
    m_b = np.where(np.abs(q - k) <= 128, 0.0, NEG)
    start = np.clip(q % 64 - 8, 0, 64 - 16)
    m_c = np.where((k % 64 >= start) & (k % 64 < start + 16), 0.0, NEG)
    tiled = [m.reshape(TT, P, T).transpose(1, 0, 2).reshape(P, TT * T).astype(f32) for m in (m_a, m_b, m_c)]
    return np.ascontiguousarray(np.concatenate(
        [np.cos(four), np.sin(four), swap, np.eye(P, dtype=f32), np.ones((P, P), f32), *tiled], 1).astype(f32))


def _chunks(w):
    n = w.shape[1] // P
    return w.reshape(2, 8, P, n, P).transpose(3, 0, 2, 1, 4).reshape(n, 2, P, PIECE)


def kernel(**inputs):
    import concourse.bacc as bacc
    from concourse.bass_utils import run_bass_kernel_spmd

    a = {k: np.asarray(v_) for k, v_ in inputs.items()}
    heads_b = [j + h * PB for j in range(PB) for h in range(HKV)]
    w_main, w_up, w_down, params, biases = [], [], [], [], []
    at = np.cumsum([0, WA, WA, WA, WB, WKV, WKV, WC, WC, WC])
    row = np.arange(T)
    cols_off = np.clip(row[None, :] % 64 - row[:, None] % 64 + 15, 0, 30)
    rows_off = row[None, :] // 64 - row[:, None] // 64 + 7
    for l in range(DEPTH):
        qa, ka, va, qb, kb, vb, qc, kc, vc = (a["w_in"][l][:, at[i]:at[i + 1]] for i in range(9))
        qb = qb.reshape(D, HB, HD)[:, heads_b].reshape(D, WB)
        wv = np.concatenate([va, vb, vc], 1)
        v_pieces = wv.reshape(8, 2, P, NVB, 512).transpose(3, 0, 2, 1, 4).reshape(-1, P, PIECE)

        def by_turns(wq, wk):
            return np.stack([_chunks(wq), _chunks(wk)], 1).reshape(-1, P, PIECE)

        order = [slice(0, WA), None, slice(WA + WB, D)]
        wo = a["w_out"][l]
        wo_b = wo[WA:WA + WB].reshape(HB, HD, D)[heads_b].reshape(WB, D)
        wo = np.concatenate([wo[order[0]], wo_b, wo[order[2]]], 0)
        mg = a["mix_gain"][l]
        mg = np.concatenate([mg[:WA], mg[WA:WA + WB].reshape(HB, HD)[heads_b].reshape(-1), mg[WA + WB:]])
        w_main.append(np.concatenate([
            v_pieces, by_turns(qa, ka), _chunks(np.concatenate([kb, qb], 1)).reshape(-1, P, PIECE),
            by_turns(qc, kc), _chunks(wo).reshape(-1, P, PIECE)]).reshape(MAIN, RING, P, PIECE))
        up = a["w_up"][l]
        w_up.append(by_turns(up[:, :D_FF], up[:, D_FF:]).reshape(FC, RING, P, PIECE))
        w_down.append(a["w_down"][l].reshape(QUARTERS, FQ, P, KC, P).transpose(0, 3, 2, 1, 4)
                      .reshape(QUARTERS * G_DOWN, RING, P, PIECE_DOWN))
        conv = np.concatenate([a["conv_w"][l], a["conv_b"][l][None]], 0).reshape(4, 2, FC, P)
        params += [a["ln_attn"][l].reshape(KC, P).T, mg.reshape(KC, P).T, a["ln_ffn"][l].reshape(KC, P).T,
                   conv.transpose(3, 2, 1, 0).reshape(P, 8 * FC),
                   np.broadcast_to(a["sink_b"][l][heads_b], (P, HB))]
        rpb = a["rpb_c"][l][:, rows_off, cols_off]
        biases.append(rpb.reshape(HC, TT, P, T).transpose(2, 0, 1, 3).reshape(P, HC, TT * T))
    params.append(a["ln_final"].reshape(KC, P).T)
    arrays = {
        "in_x": a["x"][0].reshape(T, KC, P).transpose(2, 1, 0),
        "in_w_main": np.stack(w_main).reshape(DEPTH * MAIN, RING, P, PIECE),
        "in_w_up": np.stack(w_up).reshape(DEPTH * FC, RING, P, PIECE),
        "in_w_down": np.stack(w_down).reshape(DEPTH * QUARTERS * G_DOWN, RING, P, PIECE_DOWN),
        "in_bias_c": np.stack(biases),
        "in_params": np.concatenate(params, 1),
        "in_consts": _constants(),
    }
    arrays = {k: np.ascontiguousarray(v_) for k, v_ in arrays.items()}
    nc = bacc.Bacc("TRN2", target_bir_lowering=False, num_devices=1)
    args = [nc.dram_tensor(n, v_.shape, F32, kind="ExternalInput").ap() for n, v_ in arrays.items()]
    args.append(nc.dram_tensor("out_y", (P, KC, T), F32, kind="ExternalOutput").ap())
    build(nc, *args)
    r = run_bass_kernel_spmd(nc, [arrays], core_ids=[0])
    y = np.asarray(r.results[0]["out_y"])
    return y.transpose(2, 1, 0).reshape(1, T, D)
```

```python
from contextlib import ExitStack

import numpy as np
import concourse.bass as bass
from concourse import mybir

P = 128
F32 = mybir.dt.float32
F32R = mybir.dt.float32r
ALU = mybir.AluOpType
ACT = mybir.ActivationFunctionType

DEPTH, D, T, HD, D_FF = 2, 2048, 256, 64, 5632
HA, HB, HC, HKV = 12, 10, 10, 2
WA, WB, WKV, WC = HA * HD, HB * HD, HKV * HD, HC * HD
VCOLS = WA + WKV + WC
EPS = 1e-6
NEG = -1e30

KC = D // P
TT = T // P
NVB = VCOLS // 512
FC = D_FF // P
QUARTERS = 4
FQ = FC // QUARTERS

PA, PB, PC = HA // 2, HB // 2, HC // 2
PAIRS = PA + PB + PC
ROT = 2 * PA + 1 + PB
QK = ROT + 2 * PC
XPARTS = 8
SQ_POOL = 10
Y_POOL = KC - 5
BRANCHES = ((0, WA), (WA, WB), (WA + WB, WC))

RING = 4
PIECE = 8 * P
PIECE_DOWN = FQ * P
G_V, G_PROJ, G_OUT, G_FFN = 0, 2 * NVB, 2 * NVB + 14, 2 * NVB + 14 + KC // 2
G_UP, G_DOWN = FQ, KC // 4
G_QUARTER = G_UP + G_DOWN
GROUPS = G_FFN + QUARTERS * G_QUARTER
MAIN = G_FFN

R_V, R_PROJ, R_OUT = 0, NVB, NVB + 14
R_FFN = R_OUT + KC // 2
R_QUARTER = FQ + KC // 2
ROUNDS = R_FFN + QUARTERS * R_QUARTER

O_LN1, O_MIX, O_LN2, O_CONV, O_SINK = 0, KC, 2 * KC, 3 * KC, 3 * KC + 8 * FC
NPAR = O_SINK + HB
O_COS, O_SIN, O_ROT, O_ID, O_ONE = 0, T, 2 * T, 2 * T + P, 2 * T + 2 * P
O_MASK = 2 * T + 3 * P
NCONST = O_MASK + 3 * TT * T

SEED_SLOT = RING
SEED_ACC = 1
SEED_SCORES = 1
SEED_HEAD = 2
SEED_PAIR = 1
SEED_ROT = 2
SEED_ROT_READ = 1
SEED_QK = 1
SEED_PROD = 1
SEED_SQ = 1
SEED_CONV = 2


def build(nc, xT, w_main, w_up, w_down, bias_c, params, consts, outT):
    with ExitStack() as ctx:
        def sb(name, shape, dt=F32):
            return ctx.enter_context(nc.sbuf_tensor(name, shape, dt))

        def bank(name):
            return ctx.enter_context(nc.psum_tensor(name, [P, 512], F32))

        def sem(name):
            return ctx.enter_context(nc.semaphore(name))

        acc = [bank("acc0"), bank("acc1")]
        aux = bank("aux")
        scores_ps = [bank("scores0"), bank("scores1")]
        pt_ps = [bank("pt0"), bank("pt1")]
        o_ps = bank("o_ps")

        x = sb("x", [P, KC, T])
        h_hi, h_lo = sb("h_hi", [P, KC, T], F32R), sb("h_lo", [P, KC, T], F32R)
        with nc.sbuf_tensor("mixed", [P, TT, D], F32) as mixed:
            pass
        h2_hi = sb("h2_hi", [P, KC, T], F32R)
        with nc.sbuf_tensor("v", [P, TT, VCOLS], F32) as v, nc.sbuf_tensor("pt_sb", [P, 2, TT * T], F32) as pt_sb:
            pass
        h2_lo = sb("h2_lo", [P, KC, T], F32R)
        as_chunks = mixed.ap().rearrange("p t (k c) -> p (t k) c", c=T)
        w_raw = sb("w_raw", [P, RING, PIECE_DOWN])
        w_hi = [sb(f"w_hi{s}", [P, PIECE_DOWN], F32R) for s in range(RING)]
        w_lo = [sb(f"w_lo{s}", [P, PIECE_DOWN], F32R) for s in range(RING)]
        with nc.sbuf_tensor("bias", [P, HC, TT * T], F32) as bias:
            pass
        act_hi, act_lo = sb("act_hi", [P, FQ, T], F32R), sb("act_lo", [P, FQ, T], F32R)
        par = sb("par", [P, DEPTH * NPAR + KC])
        con = sb("con", [P, NCONST])
        raw = [sb("raw0", [P, T]), sb("raw1", [P, T])]
        with nc.sbuf_tensor("raw_hi", [P, 2, T], F32R) as raw_hi:
            pass
        z = sb("z", [P, 2, T])
        raw_lo = sb("raw_lo", [P, 2, T], F32R)
        rot_r = sb("rot_r", [P, P], F32R)
        qk = sb("qk", [P, T])
        q_hi, q_lo, k_hi, k_lo = (sb(n, [P, T], F32R) for n in ("q_hi", "q_lo", "k_hi", "k_lo"))
        rot_sin, rot_cos = sb("rot_sin", [P, T]), sb("rot_cos", [P, T])
        with nc.sbuf_tensor("s_sb", [P, 2, TT * T], F32) as s_sb:
            pass
        gate, value = sb("gate", [P, T]), sb("value", [P, T])
        silu, prod = sb("silu", [P, T]), sb("prod", [P, T])
        junk = sb("junk", [P, WA])
        mx, nmx = sb("mx", [P, 4]), sb("nmx", [P, 4])
        den, esink, den_all, rden = (sb(n, [P, 4]) for n in ("den", "esink", "den_all", "rden"))
        branch_ssq, branch_ms, branch_r = (sb(n, [P, 4, TT]) for n in ("branch_ssq", "branch_ms", "branch_r"))
        sq, sq_sum = sb("sq", [P, T]), sb("sq_sum", [P, T])
        ms, r_tok = sb("ms", [P, TT]), sb("r_tok", [P, TT])
        r_all = sb("r_all", [P, T])
        silu_first = sb("silu_first", [P, TT])
        minus_half, zeros = sb("minus_half", [P, TT]), sb("zeros", [P, T])
        diag = sb("diag", [P, TT, P])

        cos, sin = con[:, O_COS:O_COS + T], con[:, O_SIN:O_SIN + T]
        rot_m, ident, ones = (con[:, o:o + P] for o in (O_ROT, O_ID, O_ONE))
        mask_a, mask_b, mask_c = (con[:, O_MASK + b * TT * T:O_MASK + (b + 1) * TT * T] for b in range(3))

        landed = [sem(f"landed{s}") for s in range(RING)]
        x_landed = [sem(f"x_landed{i}") for i in range(XPARTS)]
        par_landed, id_landed, con_landed, mask_landed, bias_landed, stored = (
            sem(n) for n in ("par_landed", "id_landed", "con_landed", "mask_landed", "bias_landed",
                             "stored"))
        slot_used, v_tile0, rot_ready, scores_ready, transposed, pv_done, ssq_ready, r_ready, mixt_ready = (
            sem(n) for n in ("slot_used", "v_tile0", "rot_ready", "scores_ready", "transposed", "pv_done",
                             "ssq_ready", "r_ready", "mixt_ready"))
        hi_done, exp_done, pt_ready, h_hi_done, branch_sq, mix_hi_done, affine_done, silu_done, act_hi_done = (
            sem(n) for n in ("hi_done", "exp_done", "pt_ready", "h_hi_done", "branch_sq", "mix_hi_done",
                             "affine_done", "silu_done", "act_hi_done"))
        split_done, rot_read, rot_done, masked, maxed, den_done, recip_done, mixed_done = (
            sem(n) for n in ("split_done", "rot_read", "rot_done", "masked", "maxed", "den_done", "recip_done",
                             "mixed_done"))
        ms_done, diag_done, r_all_done, h_lo_done, mix_lo_done, y_done = (
            sem(n) for n in ("ms_done", "diag_done", "r_all_done", "h_lo_done", "mix_lo_done", "y_done"))
        branch_ms_done, branch_scaled, tap_done, conv_done = (
            sem(n) for n in ("branch_ms_done", "branch_scaled", "tap_done", "conv_done"))
        raw_hi_done, qk_hi_done, qk_done = sem("raw_hi_done"), sem("qk_hi_done"), sem("qk_done")
        cos_done, bias_ready, sq_done, sum_done, r_tok_done, branch_r_done, prod_done, act_lo_done = (
            sem(n) for n in ("cos_done", "bias_ready", "sq_done", "sum_done", "r_tok_done", "branch_r_done",
                             "prod_done", "act_lo_done"))
        raw_lo_done, rot_r_set = sem("raw_lo_done"), sem("rot_r_set")
        scaled_done, y_pool_done = sem("scaled_done"), sem("y_pool_done")
        first_squares = sem("first_squares")
        half_set, zeros_set, mask_begun = sem("half_set"), sem("zeros_set"), sem("mask_begun")
        acc_free = [sem("acc_free0"), sem("acc_free1")]

        def par_col(l, col):
            return par[:, bass.ds(l * NPAR + col, 1)]

        def mix_place(c):
            return (aux, scores_ps[0], scores_ps[1])[c % 3][:, 0:T]

        block = ctx.enter_context(nc.Block())

        @block.sync
        def _(sp):
            def load(g, s, src, cols):
                sp.wait_ge(split_done, RING * g + s + 1)
                sp.dma_start(w_raw[:, s, 0:cols], src).then_inc(landed[s], 16)

            for i in range(XPARTS):
                c = slice(i * KC // XPARTS, (i + 1) * KC // XPARTS)
                sp.dma_start(x[:, c], xT[:, c]).then_inc(x_landed[i], 16)
                if i == 0:
                    sp.dma_start(par[:], params).then_inc(par_landed, 16)
                if i < RING:
                    load(0, i, w_main[0, i], PIECE)
            sp.dma_start(con[:, O_ID:O_MASK], consts[:, O_ID:O_MASK]).then_inc(id_landed, 16)
            with sp.Fori(0, DEPTH) as l:
                with sp.If(l > 0):
                    for s in range(RING):
                        load(l * GROUPS, s, w_main[bass.ds(l * MAIN, 1), s].rearrange("a p c -> (a p) c"), PIECE)
                with sp.Fori(1, MAIN) as i:
                    for s in range(RING):
                        load(l * GROUPS + i, s, w_main[bass.ds(l * MAIN + i, 1), s].rearrange("a p c -> (a p) c"), PIECE)
                with sp.Fori(0, QUARTERS) as q:
                    with sp.Fori(0, G_UP) as i:
                        for s in range(RING):
                            load(l * GROUPS + q * G_QUARTER + i + G_FFN, s,
                                 w_up[bass.ds(l * FC + q * FQ + i, 1), s].rearrange("a p c -> (a p) c"), PIECE)
                    with sp.Fori(0, G_DOWN) as i:
                        for s in range(RING):
                            load(l * GROUPS + q * G_QUARTER + i + (G_FFN + G_UP), s,
                                 w_down[bass.ds(l * (QUARTERS * G_DOWN) + q * G_DOWN + i, 1), s].rearrange("a p c -> (a p) c"),
                                 PIECE_DOWN)
            sp.wait_ge(y_done, Y_POOL // 2)
            sp.dma_start(outT[:, 0:Y_POOL // 2], as_chunks[:, 0:Y_POOL // 2]).then_inc(stored, 16)
            sp.wait_ge(y_done, Y_POOL)
            sp.dma_start(outT[:, Y_POOL // 2:Y_POOL], as_chunks[:, Y_POOL // 2:Y_POOL]).then_inc(stored, 16)
            sp.wait_ge(y_pool_done, KC - Y_POOL)
            sp.dma_start(outT[:, Y_POOL:KC], as_chunks[:, Y_POOL:KC]).then_inc(stored, 16)
            sp.wait_ge(stored, 3 * 16)

        @block.tensor
        def _(pe):
            def mm3(out, hi, lo, start, stop, stationary_hi, stationary_lo):
                pe.matmul(out, stationary_hi, hi, start=start, stop=False)
                pe.matmul(out, stationary_hi, lo, start=False, stop=False)
                return pe.matmul(out, stationary_lo, hi, start=False, stop=stop)

            def piece_split(g, s):
                pe.wait_ge(split_done, RING * g + s + (SEED_SLOT + 1))

            def acc_taken(l, rnd, b):
                pe.wait_ge(acc_free[b], l * ROUNDS + rnd + SEED_ACC)

            def chunk(l, g, s0, rnd, b, hi=h_hi, lo=h_lo, before=None):
                acc_taken(l, rnd, b)
                for k in range(KC):
                    s, kk = s0 + k // 8, k % 8
                    if kk == 0:
                        piece_split(g, s)
                    if before:
                        before(k)
                    w = slice(kk * P, (kk + 1) * P)
                    last = mm3(acc[b][:, 0:T], hi[:, k], lo[:, k], k == 0, k == KC - 1, w_hi[s][:, w], w_lo[s][:, w])
                    if kk == 7:
                        last.then_inc(slot_used, 1)

            def two_chunks(l, g, rnd, ks, before=None):
                if ks[0] == 0:
                    acc_taken(l, rnd, 0)
                    acc_taken(l, rnd, 1)
                for k in ks:
                    if before:
                        before(k)
                    for b in range(2):
                        s, kk = 2 * b + k // 8, k % 8
                        if kk == 0:
                            piece_split(g, s)
                        w = slice(kk * P, (kk + 1) * P)
                        out = acc[b][:, 0:T]
                        pe.matmul(out, w_hi[s][:, w], h_hi[:, k], start=k == 0, stop=False)
                        mid = pe.matmul(out, w_hi[s][:, w], h_lo[:, k], start=False, stop=False)
                        last = pe.matmul(out, w_lo[s][:, w], h_hi[:, k], start=False, stop=k == KC - 1)
                        if kk == 7 and b == 0:
                            last.then_inc(slot_used, 1)
                        if k == KC - 1 and b == 1:
                            mid.then_inc(slot_used, 1)
                            last.then_inc(slot_used, 1)

            def norm_sum(n):
                pe.wait_ge(sum_done, n * (KC + 1) + (KC + 1))
                pe.wait_ge(id_landed, 16)
                for t in range(TT):
                    last = pe.matmul(aux[:, T + t:T + t + 1], sq_sum[:, t * P:(t + 1) * P], ones[:, 0:1],
                                     start=True, stop=True)
                last.then_inc(ssq_ready, 1)

            def norm_spread(n):
                for t in range(TT):
                    pe.wait_ge(diag_done, 2 * n + t + 1)
                    last = pe.matmul(aux[:, t * P:(t + 1) * P], ones, diag[:, t], start=True, stop=True)
                last.then_inc(r_ready, 1)

            def rotate(l, i, b):
                pe.wait_ge(raw_lo_done, l * ROT + 2 * i + (b + 1))
                pe.wait_ge(rot_read, l * ROT + 2 * i + (b + SEED_ROT_READ))
                pe.matmul(aux[:, 0:T], rot_r[:], raw_hi[:, b], start=True, stop=False)
                pe.matmul(aux[:, 0:T], rot_r[:], raw_lo[:, b], start=False, stop=True).then_inc(rot_ready, 1)

            def scores(l, pair):
                for hh in range(2):
                    pe.wait_ge(masked, l * (2 * PAIRS) + 2 * pair + (hh - 1 + SEED_HEAD))
                    rows = slice(hh * HD, (hh + 1) * HD)
                    for t in range(TT):
                        tok = slice(t * P, (t + 1) * P)
                        last = mm3(scores_ps[hh][:, t * T:(t + 1) * T], k_hi[rows, :], k_lo[rows, :], True, True,
                                   q_hi[rows, tok], q_lo[rows, tok])
                    last.then_inc(scores_ready, 1)

            def transposes(l, pair):
                for hh in range(2):
                    pe.wait_ge(exp_done, l * (2 * PAIRS) + 2 * pair + (hh + 1))
                    pe.wait_ge(pt_ready, l * (2 * PAIRS) + 2 * pair + (hh - 1 + SEED_HEAD))
                    for kb in range(TT):
                        for t in range(TT):
                            last = pe.transpose(pt_ps[hh][:, kb * T + t * P:kb * T + (t + 1) * P],
                                                s_sb[:, hh, t * T + kb * P:t * T + (kb + 1) * P], ident)
                    last.then_inc(transposed, 1)

            def values(l, pair, vcol):
                pe.wait_ge(mixed_done, l * PAIRS + pair + SEED_PAIR)
                for hh in range(2):
                    pe.wait_ge(pt_ready, l * (2 * PAIRS) + 2 * pair + (hh + 1 + SEED_HEAD))
                    for t in range(TT):
                        for kb in range(TT):
                            last = pe.matmul(o_ps[:, (hh * TT + t) * HD:(hh * TT + t + 1) * HD],
                                             pt_sb[:, hh, kb * T + t * P:kb * T + (t + 1) * P],
                                             v[:, kb, bass.ds(vcol + hh * HD, HD)], start=kb == 0, stop=kb == TT - 1)
                last.then_inc(pv_done, 1)

            def mix_t(l, c):
                if c in (1, 2):
                    pe.wait_ge(masked, l * (2 * PAIRS) + (2 * PAIRS + c - 2 + SEED_HEAD))
                for t in range(TT):
                    last = pe.transpose(mix_place(c)[:, t * P:(t + 1) * P], mixed[:, t, c * P:(c + 1) * P], ident)
                last.then_inc(mixt_ready, 1)

            with pe.Fori(0, DEPTH) as l:
                lg = l * GROUPS
                def v_block(blk, first):
                    for half in range(2):
                        for s in range(RING):
                            if first and half == 1 and s == 3:
                                norm_sum(2 * l)
                            piece_split(lg + 2 * blk + half, s)
                            for t in range(TT):
                                if half == 0 and s == 0:
                                    acc_taken(l, blk, t)
                                for kk in range(2):
                                    k = half * 8 + s * 2 + kk
                                    if t == 0 and first:
                                        pe.wait_ge(h_lo_done, l * (2 * KC) + (k + 1))
                                    cols = slice(kk * 512, (kk + 1) * 512)
                                    tok = slice(t * P, (t + 1) * P)
                                    pe.matmul(acc[t][:], h_hi[:, k, tok], w_hi[s][:, cols], start=k == 0, stop=False)
                                    pe.matmul(acc[t][:], h_hi[:, k, tok], w_lo[s][:, cols], start=False, stop=False)
                                    last = pe.matmul(acc[t][:], h_lo[:, k, tok], w_hi[s][:, cols], start=False,
                                                     stop=k == KC - 1)
                                if k == KC - 1 and t == 0:
                                    last.then_inc(v_tile0, 1)
                            last.then_inc(slot_used, 1)

                v_block(0, True)
                norm_spread(2 * l)
                with pe.Fori(1, NVB) as blk:
                    v_block(blk, False)
                pe.wait_ge(rot_r_set, 1)
                def step_a(i, pairs_before):
                    chunk(l, lg + i + G_PROJ, 0, i + R_PROJ, 0)
                    if pairs_before >= 1:
                        rotate(l, i - 1, 1)
                    if pairs_before >= 2:
                        transposes(l, i - 2)
                    chunk(l, lg + i + G_PROJ, 2, i + R_PROJ, 1)
                    if pairs_before >= 2:
                        values(l, i - 2, (i - 2) * P)
                    if pairs_before >= 1:
                        pe.wait_ge(qk_done, l * QK + 2 * i + SEED_QK)
                        scores(l, i - 1)
                    rotate(l, i, 0)

                step_a(0, 0)
                step_a(1, 1)
                with pe.Fori(2, PA) as i:
                    step_a(i, 2)

                chunk(l, lg + G_PROJ + PA, 0, R_PROJ + PA, 0)
                rotate(l, PA - 1, 1)
                transposes(l, PA - 2)
                chunk(l, lg + G_PROJ + PA, 2, R_PROJ + PA, 1)
                values(l, PA - 2, (PA - 2) * P)
                pe.wait_ge(qk_done, l * QK + 2 * PA + SEED_QK)
                scores(l, PA - 1)
                rotate(l, PA, 0)

                def rotate_first_q(k):
                    if k == 8:
                        rotate(l, PA, 1)

                for j in range(1, PB):
                    r = 2 * PA + 1 + j
                    pair = PA + j
                    chunk(l, lg + G_PROJ + r // 2, 2 * (r % 2), R_PROJ + r // 2, r % 2,
                          before=rotate_first_q if j == 1 else None)
                    transposes(l, pair - 2)
                    pe.wait_ge(qk_done, l * QK + r + SEED_QK)
                    scores(l, pair - 1)
                    rotate(l, r // 2, r % 2)
                    values(l, pair - 2, (PA - 1) * P if j == 1 else WA)

                def step_c(i):
                    pair, at = PA + PB + i, PA + 3 + i
                    chunk(l, lg + G_PROJ + at, 0, R_PROJ + at, 0)
                    transposes(l, pair - 2)
                    pe.wait_ge(qk_done, l * QK + (ROT + 2 * i + SEED_QK))
                    scores(l, pair - 1)
                    chunk(l, lg + G_PROJ + at, 2, R_PROJ + at, 1)
                    values(l, pair - 2, WA if i < 2 else WA + WKV + (i - 2) * P)

                for i in range(PC):
                    step_c(i)

                def mix_ready(k):
                    pe.wait_ge(mix_lo_done, l * KC + (k + 1))

                def out_and_mix(k):
                    two_chunks(l, lg + G_OUT, R_OUT, [k], mix_ready)
                    if k + 3 in (PA, PA + PB):
                        pe.wait_ge(branch_scaled, 3 * l + (2 if k + 3 == PA else 3))
                    if k + 3 < KC:
                        mix_t(l, k + 3)

                transposes(l, PAIRS - 2)
                pe.wait_ge(qk_done, l * QK + (QK + SEED_QK))
                scores(l, PAIRS - 1)
                values(l, PAIRS - 2, WA + WKV + (PC - 2) * P)
                pe.wait_ge(branch_scaled, 3 * l + 1)
                for c in range(3):
                    mix_t(l, c)
                transposes(l, PAIRS - 1)
                out_and_mix(0)
                out_and_mix(1)
                values(l, PAIRS - 1, WA + WKV + (PC - 1) * P)
                for k in range(2, KC):
                    out_and_mix(k)

                with pe.Fori(1, KC // 2) as i:
                    chunk(l, lg + i + G_OUT, 0, i + R_OUT, 0)
                    chunk(l, lg + i + G_OUT, 2, i + R_OUT, 1)

                def h2_ready(k):
                    pe.wait_ge(h_lo_done, l * (2 * KC) + (KC + k + 1))
                    if k == 8:
                        norm_sum(2 * l + 1)

                def spread(k):
                    if k == 0:
                        norm_spread(2 * l + 1)

                def quarter(q, first):
                    g0, r0 = lg + q * G_QUARTER, q * R_QUARTER
                    chunk(l, g0 + G_FFN, 0, r0 + R_FFN, 0, h2_hi, h2_lo, h2_ready if first else None)
                    chunk(l, g0 + G_FFN, 2, r0 + R_FFN, 1, h2_hi, h2_lo, spread if first else None)
                    with pe.Fori(1, FQ) as j:
                        chunk(l, g0 + j + G_FFN, 0, r0 + j + R_FFN, 0, h2_hi, h2_lo)
                        chunk(l, g0 + j + G_FFN, 2, r0 + j + R_FFN, 1, h2_hi, h2_lo)

                    def down_products(s, ks):
                        for k in ks:
                            w = slice(k * P, (k + 1) * P)
                            last = mm3(acc[s % 2][:, 0:T], act_hi[:, k], act_lo[:, k], k == 0, k == FQ - 1,
                                       w_hi[s][:, w], w_lo[s][:, w])
                        return last

                    def down_begin(i, s):
                        acc_taken(l, r0 + 2 * i + (R_FFN + FQ + s // 2), s % 2)
                        piece_split(g0 + i + (G_FFN + G_UP), s)

                    split_at = (FQ - 1, FQ - 3)
                    for s in range(2):
                        down_begin(0, s)
                        if s == 0:
                            pe.wait_ge(act_lo_done, l * FC + q * FQ + (FQ - 1 + SEED_PROD))
                        down_products(s, range(split_at[s]))
                    pe.wait_ge(act_lo_done, l * FC + q * FQ + (FQ + SEED_PROD))
                    for s in range(2):
                        down_products(s, range(split_at[s], FQ)).then_inc(slot_used, 1)
                    for s in range(2, RING):
                        down_begin(0, s)
                        down_products(s, range(FQ)).then_inc(slot_used, 1)
                    with pe.Fori(1, G_DOWN) as i:
                        for s in range(RING):
                            down_begin(i, s)
                            down_products(s, range(FQ)).then_inc(slot_used, 1)

                quarter(0, True)
                with pe.Fori(1, QUARTERS) as q:
                    quarter(q, False)
            norm_sum(2 * DEPTH)
            norm_spread(2 * DEPTH)

        @block.scalar
        def _(act):
            def hi(g, s, cols=PIECE):
                act.wait_ge(landed[s], 16 * g + 16)
                act.wait_ge(slot_used, RING * g + s + 1)
                act.activation(w_hi[s][:, 0:cols], w_raw[:, s, 0:cols], ACT.Copy).then_inc(hi_done, 1)

            def h_chunk_hi(c, to, gain):
                act.activation(to[:, bass.ds(c, 1)].rearrange("p a t -> p (a t)"),
                               x[:, bass.ds(c, 1)].rearrange("p a t -> p (a t)"), ACT.Copy,
                               scale=gain).then_inc(h_hi_done, 1)

            def copy_pt(l, pair):
                for hh in range(2):
                    act.wait_ge(transposed, l * (2 * PAIRS) + 2 * pair + (hh + 1 + SEED_HEAD))
                    act.wait_ge(pv_done, l * PAIRS + pair + SEED_PAIR)
                    act.activation(pt_sb[:, hh], pt_ps[hh][:], ACT.Copy).then_inc(pt_ready, 1)

            def exps(l, pair, sink=None):
                act.wait_ge(recip_done, l * PAIRS + pair + SEED_PAIR)
                for hh in range(2):
                    act.wait_ge(maxed, l * (2 * PAIRS) + 2 * pair + (hh + 1))
                    if sink is not None:
                        act.activation(esink[:, 2 * hh:2 * hh + 2], nmx[:, 2 * hh:2 * hh + 2], ACT.Exp,
                                       bias=par_col(l, O_SINK + 2 * sink + hh))
                    for t in range(TT):
                        at = slice(t * T, (t + 1) * T)
                        last = act.activation(s_sb[:, hh, at], s_sb[:, hh, at], ACT.Exp,
                                              bias=nmx[:, 2 * hh + t:2 * hh + t + 1],
                                              accum_out=den[:, 2 * hh + t:2 * hh + t + 1])
                    last.then_inc(exp_done, 1)

            def branch_squares(l, part):
                first, end = (0, PA, PA + PB, PAIRS - 1, PAIRS)[part:part + 2]
                act.wait_ge(mixed_done, l * PAIRS + (end + SEED_PAIR))
                for t in range(TT):
                    act.wait_ge(branch_sq, 4 * TT * l + (TT * part + t + SEED_SQ))
                    act.activation(junk[:, 0:(end - first) * P], mixed[:, t, first * P:end * P], ACT.Square,
                                   accum_out=branch_ssq[:, part, t:t + 1]).then_inc(branch_sq, 1)

            def mix_hi(l, c):
                act.wait_ge(mixt_ready, l * KC + (c + 1))
                act.activation(h_hi[:, c], mix_place(c), ACT.Copy,
                               scale=par_col(l, O_MIX + c)).then_inc(mix_hi_done, 1)

            act.wait_ge(half_set, 1)
            act.activation(silu_first[:], minus_half[:], ACT.Copy)
            act.wait_ge(par_landed, 16)
            for i in range(XPARTS):
                act.wait_ge(x_landed[i], 16)
                for c in range(i * KC // XPARTS, (i + 1) * KC // XPARTS):
                    h_chunk_hi(c, h_hi, par[:, O_LN1 + c:O_LN1 + c + 1])
                if i < RING:
                    hi(0, i)
            for c in range(SQ_POOL, KC):
                act.activation(as_chunks[:, c], x[:, c], ACT.Square).then_inc(first_squares, 1)
            with act.Fori(0, DEPTH) as l:
                lg = l * GROUPS
                with act.Fori(0, NVB) as blk:
                    for s in range(RING):
                        hi(lg + 2 * blk + 1, s)
                    for s in range(RING - 1):
                        hi(lg + 2 * blk + 2, s)
                    act.wait_ge(r_tok_done, 2 * l + 1)
                    act.wait_ge(v_tile0, NVB * l + blk + 1)
                    act.activation(v[:, 0, bass.ds(blk * 512, 512)], acc[0][:], ACT.Copy,
                                   scale=r_tok[:, 0:1]).then_inc(acc_free[0], 1)
                    act.wait_ge(slot_used, RING * (lg + 2 * blk + 1) + (RING + SEED_SLOT))
                    act.activation(v[:, 1, bass.ds(blk * 512, 512)], acc[1][:], ACT.Copy,
                                   scale=r_tok[:, 1:2]).then_inc(acc_free[1], 1)
                    hi(lg + 2 * blk + 2, RING - 1)

                def step_a(i, pairs_before):
                    g = lg + i + (G_PROJ + 1)
                    hi(g, 0)
                    hi(g, 1)
                    if pairs_before >= 2:
                        copy_pt(l, i - 2)
                    hi(g, 2)
                    hi(g, 3)
                    if pairs_before >= 1:
                        exps(l, i - 1)

                step_a(0, 0)
                step_a(1, 1)
                with act.Fori(2, PA) as i:
                    step_a(i, 2)
                g = lg + (G_PROJ + PA + 1)
                hi(g, 0)
                hi(g, 1)
                copy_pt(l, PA - 2)
                hi(g, 2)
                hi(g, 3)
                exps(l, PA - 1)
                for j in range(1, PB):
                    r = 2 * PA + 1 + j
                    g = lg + (G_PROJ + r // 2 + 1)
                    hi(g, 2 * (r % 2))
                    hi(g, 2 * (r % 2) + 1)
                    copy_pt(l, PA + j - 2)
                    exps(l, PA + j - 1, sink=j - 1)
                for i in range(PC):
                    g = lg + (G_PROJ + PA + 3 + i + 1)
                    pair = PA + PB + i
                    hi(g, 0)
                    hi(g, 1)
                    copy_pt(l, pair - 2)
                    hi(g, 2)
                    exps(l, pair - 1, sink=PB - 1 if i == 0 else None)
                    hi(g, 3)
                    if i == 1:
                        branch_squares(l, 0)
                    if i == 3:
                        branch_squares(l, 1)
                copy_pt(l, PAIRS - 2)
                exps(l, PAIRS - 1)
                for c in range(3):
                    mix_hi(l, c)
                copy_pt(l, PAIRS - 1)
                branch_squares(l, 2)
                mix_hi(l, 3)
                mix_hi(l, 4)
                branch_squares(l, 3)
                for c in range(5, KC):
                    mix_hi(l, c)
                    if c == 8:
                        act.activation(silu_first[:], minus_half[:], ACT.Silu)
                    if c == 11:
                        hi(lg + (G_OUT + 1), 0)
                def out_chunks(i, first):
                    for b in range(2):
                        if not (first and b == 0):
                            hi(lg + i + (G_OUT + 1), 2 * b)
                        hi(lg + i + (G_OUT + 1), 2 * b + 1)
                        act.wait_ge(acc_free[b], l * ROUNDS + i + (R_OUT + SEED_ACC + 1))
                        h_chunk_hi(2 * i + b, h2_hi, par[:, bass.ds(l * NPAR + 2 * i + (O_LN2 + b), 1)])

                out_chunks(0, True)
                with act.Fori(1, KC // 2) as i:
                    out_chunks(i, False)

                def quarter(q, last):
                    g0 = lg + q * G_QUARTER

                    def product_hi(j):
                        act.wait_ge(prod_done, l * FC + q * FQ + j + (SEED_PROD + 1))
                        act.activation(act_hi[:, bass.ds(j, 1)].rearrange("p a t -> p (a t)"), prod[:],
                                       ACT.Copy).then_inc(act_hi_done, 1)

                    def up(j, cols, first=False):
                        g = g0 + j + (G_FFN + 1)
                        f = q * FQ + j
                        col = l * NPAR + 8 * f
                        hi(g, 0, cols)
                        if not first:
                            product_hi(j - 1)
                        hi(g, 1, cols)
                        act.wait_ge(acc_free[0], l * ROUNDS + q * R_QUARTER + j + (R_FFN + SEED_ACC + 1))
                        act.activation(gate[:], z[:, 0], ACT.Identity,
                                       scale=par[:, bass.ds(col + (O_CONV + 1), 1)],
                                       bias=par[:, bass.ds(col + (O_CONV + 3), 1)]).then_inc(affine_done, 1)
                        hi(g, 2, cols)
                        act.wait_ge(conv_done, l * (2 * FC) + 2 * f + (1 + SEED_CONV))
                        act.wait_ge(prod_done, l * FC + f + SEED_PROD)
                        act.activation(silu[:], gate[:], ACT.Silu).then_inc(silu_done, 1)
                        if cols == PIECE:
                            hi(g, 3, cols)
                        act.wait_ge(acc_free[1], l * ROUNDS + q * R_QUARTER + j + (R_FFN + SEED_ACC + 1))
                        act.activation(value[:], z[:, 1], ACT.Identity,
                                       scale=par[:, bass.ds(col + (O_CONV + 5), 1)],
                                       bias=par[:, bass.ds(col + (O_CONV + 7), 1)]).then_inc(affine_done, 1)
                        if cols != PIECE:
                            hi(g, 3, cols)

                    up(0, PIECE, True)
                    with act.Fori(1, FQ - 1) as j:
                        up(j, PIECE)
                    up(FQ - 1, PIECE_DOWN)
                    product_hi(FQ - 1)

                    def down(i, s):
                        if last:
                            act.wait_ge(acc_free[s % 2], l * ROUNDS + 2 * i
                                        + (QUARTERS * R_QUARTER - R_QUARTER + R_FFN + FQ + s // 2 + SEED_ACC + 1))
                            h_chunk_hi(4 * i + s, h_hi, par[:, bass.ds(l * NPAR + 4 * i + (NPAR + O_LN1 + s), 1)])

                    with act.Fori(0, G_DOWN - 1) as i:
                        for s in range(RING):
                            hi(g0 + i + (G_FFN + G_UP + 1), s, PIECE_DOWN)
                            down(i, s)
                    if last:
                        for s in range(RING):
                            down(G_DOWN - 1, s)
                            with act.If(l < DEPTH - 1):
                                hi(g0 + (G_FFN + G_QUARTER), s)
                    else:
                        for s in range(RING):
                            hi(g0 + (G_FFN + G_QUARTER), s)

                with act.Fori(0, QUARTERS - 1) as q:
                    quarter(q, False)
                quarter(QUARTERS - 1, True)
            for c in range(Y_POOL, KC):
                act.wait_ge(acc_free[c % 2], DEPTH * ROUNDS - KC // 2 + c // 2 + SEED_ACC + 1)
                act.activation(as_chunks[:, c], x[:, c], ACT.Copy,
                               scale=par[:, DEPTH * NPAR + c:DEPTH * NPAR + c + 1]).then_inc(scaled_done, 1)

        @block.vector
        def _(dve):
            def lo(g, s, cols=PIECE):
                dve.wait_ge(hi_done, RING * g + s + 1)
                dve.tensor_tensor(w_lo[s][:, 0:cols], w_raw[:, s, 0:cols], w_hi[s][:, 0:cols].bitcast(F32),
                                  ALU.subtract).then_inc(split_done, 1)

            def norm_mean(n):
                dve.wait_ge(ssq_ready, n + 1)
                dve.tensor_scalar(ms[:], aux[:, T:T + TT], 1.0 / D, EPS, ALU.mult, ALU.add).then_inc(ms_done, 1)

            def norm_diag(n):
                dve.wait_ge(r_tok_done, n + 1)
                for t in range(TT):
                    dve.tensor_scalar(diag[:, t], ident, r_tok[:, t:t + 1], None, ALU.mult).then_inc(diag_done, 1)

            def norm_end(n):
                dve.wait_ge(r_ready, n + 1)
                dve.tensor_copy(r_all[:], aux[:, 0:T]).then_inc(r_all_done, 1)

            def h_chunk_lo(n, c, hi, lo, gain):
                dve.wait_ge(h_hi_done, n * KC + c + 1)
                at = bass.ds(c, 1)
                dve.scalar_tensor_tensor(lo[:, at].rearrange("p a t -> p (a t)"), x[:, at].rearrange("p a t -> p (a t)"),
                                         gain, hi[:, at].rearrange("p a t -> p (a t)").bitcast(F32),
                                         ALU.mult, ALU.subtract).then_inc(h_lo_done, 1)

            def take(l, i, b, to, is_q):
                dve.wait_ge(slot_used, RING * (l * GROUPS + i + G_PROJ) + (1 + 2 * b + SEED_SLOT + 1))
                dve.scalar_tensor_tensor(to[:], acc[b][:, 0:T], HD ** -0.5 if is_q else 1.0, r_all[:],
                                         ALU.mult, ALU.mult).then_inc(acc_free[b], 1)

            def take_raw(l, i, b, is_q):
                dve.wait_ge(rot_done, l * ROT + 2 * i + (b - 1 + SEED_ROT))
                take(l, i, b, raw[b], is_q)
                dve.wait_ge(acc_free[b], l * ROUNDS + i + (R_PROJ + SEED_ACC + 1))
                dve.tensor_copy(raw_hi[:, b], raw[b][:]).then_inc(raw_hi_done, 1)

            def split_qk(l, n, pair, is_q):
                dve.wait_ge(scores_ready, l * (2 * PAIRS) + 2 * pair + SEED_SCORES)
                hi, lo = (q_hi, q_lo) if is_q else (k_hi, k_lo)
                dve.tensor_copy(hi[:], qk[:]).then_inc(qk_hi_done, 1)
                dve.wait_ge(qk_hi_done, l * QK + n + 1)
                dve.tensor_tensor(lo[:], qk[:], hi[:].bitcast(F32), ALU.subtract).then_inc(qk_done, 1)

            def take_c(l, i, b):
                n = ROT + 2 * i + b
                dve.wait_ge(qk_done, l * QK + (n + SEED_QK))
                take(l, PA + 3 + i, b, qk, b == 0)
                dve.wait_ge(acc_free[b], l * ROUNDS + (i + PA + 3 + R_PROJ + SEED_ACC + 1))
                split_qk(l, n, PA + PB + i, b == 0)

            def rotated(l, i, b, pair, is_q):
                dve.wait_ge(rot_ready, l * ROT + 2 * i + (b + 1))
                dve.wait_ge(rot_done, l * ROT + 2 * i + (b + SEED_ROT))
                dve.tensor_tensor(rot_sin[:], aux[:, 0:T], sin, ALU.mult).then_inc(rot_read, 1)
                dve.wait_ge(rot_read, l * ROT + 2 * i + (b + SEED_ROT_READ + 1))
                dve.wait_ge(cos_done, l * ROT + 2 * i + (b + 1))
                dve.wait_ge(qk_done, l * QK + 2 * i + (b + SEED_QK))
                dve.tensor_tensor(qk[:], rot_sin[:], rot_cos[:], ALU.add).then_inc(rot_done, 1)
                dve.wait_ge(rot_done, l * ROT + 2 * i + (b + SEED_ROT + 1))
                split_qk(l, 2 * i + b, pair, is_q)

            def mask(l, pair, masks, sink=None):
                for hh in range(2):
                    dve.wait_ge(scores_ready, l * (2 * PAIRS) + 2 * pair + (hh + 1 + SEED_SCORES))
                    dve.wait_ge(transposed, l * (2 * PAIRS) + 2 * pair + (hh - 1 + SEED_HEAD))
                    dve.sem_inc(mask_begun, 1)
                    for t in range(TT):
                        at = slice(t * T, (t + 1) * T)
                        last = dve.tensor_tensor_reduce(s_sb[:, hh, at], scores_ps[hh][:, at], masks[hh][:, at], 1.0,
                                                        -3e38, ALU.add, ALU.max, mx[:, 2 * hh + t:2 * hh + t + 1])
                    last.then_inc(masked, 1)
                    dve.wait_ge(masked, l * (2 * PAIRS) + 2 * pair + (hh + 1 + SEED_HEAD))
                    if sink is None:
                        last = dve.tensor_scalar(nmx[:, 2 * hh:2 * hh + 2], mx[:, 2 * hh:2 * hh + 2], -1.0, None, ALU.mult)
                    else:
                        last = dve.tensor_scalar(nmx[:, 2 * hh:2 * hh + 2], mx[:, 2 * hh:2 * hh + 2],
                                                 par_col(l, O_SINK + 2 * sink + hh), -1.0, ALU.max, ALU.mult)
                    last.then_inc(maxed, 1)

            def recip(l, pair, sink=None):
                dve.wait_ge(exp_done, l * (2 * PAIRS) + 2 * pair + 2)
                total = den
                if sink is not None:
                    dve.tensor_tensor(den_all[:], den[:], esink[:], ALU.add).then_inc(den_done, 1)
                    dve.wait_ge(den_done, PB * l + (sink + 1))
                    total = den_all
                dve.wait_ge(mixed_done, l * PAIRS + pair + SEED_PAIR)
                dve.reciprocal(rden[:], total[:]).then_inc(recip_done, 1)

            def outputs(l, pair):
                dve.wait_ge(recip_done, l * PAIRS + pair + (1 + SEED_PAIR))
                dve.wait_ge(pv_done, l * PAIRS + pair + (1 + SEED_PAIR))
                to = mixed[:, :, bass.ds(pair * P, P)].rearrange("p t (h d) -> p h t d", h=2)
                dve.tensor_tensor(to, o_ps[:, 0:2 * TT * HD].rearrange("p (h t d) -> p h t d", h=2, t=TT),
                                  rden[:].rearrange("p (h t) -> p h t", h=2).unsqueeze(3).to_broadcast([P, 2, TT, HD]),
                                  ALU.mult).then_inc(mixed_done, 1)

            def branch_mean(l, br):
                w = BRANCHES[br][1]
                parts = TT * (br + 1) if br < 2 else 4 * TT
                dve.wait_ge(branch_sq, 4 * TT * l + (parts + SEED_SQ))
                if br < 2:
                    last = dve.tensor_scalar(branch_ms[:, br], branch_ssq[:, br], w * EPS, None, ALU.add)
                else:
                    last = dve.scalar_tensor_tensor(branch_ms[:, br], branch_ssq[:, 2], w * EPS, branch_ssq[:, 3],
                                                    ALU.add, ALU.add)
                last.then_inc(branch_ms_done, 1)

            def branch_scale(l, br):
                o, w = BRANCHES[br]
                dve.wait_ge(branch_r_done, 3 * l + (br + 1))
                for t in range(TT):
                    last = dve.tensor_scalar(mixed[:, t, o:o + w], mixed[:, t, o:o + w], branch_r[:, br, t:t + 1],
                                             float(w) ** 0.5, ALU.mult, ALU.mult)
                last.then_inc(branch_scaled, 1)

            def mix_lo(l, c):
                dve.wait_ge(mix_hi_done, l * KC + (c + 1))
                last = dve.scalar_tensor_tensor(h_lo[:, c], mix_place(c), par_col(l, O_MIX + c), h_hi[:, c].bitcast(F32),
                                                ALU.mult, ALU.subtract)
                last.then_inc(mix_lo_done, 1)

            def add_to_x(g, s, m, b, squared):
                dve.wait_ge(slot_used, RING * g + s + (SEED_SLOT + 1))
                dve.wait_ge(sq_done, squared)
                xm = x[:, bass.ds(m, 1)].rearrange("p a t -> p (a t)")
                dve.tensor_tensor(xm, acc[b][:, 0:T], xm, ALU.add).then_inc(acc_free[b], 1)

            for s_, n in ((slot_used, SEED_SLOT), (split_done, SEED_SLOT), (acc_free[0], SEED_ACC),
                          (acc_free[1], SEED_ACC), (scores_ready, SEED_SCORES), (transposed, SEED_HEAD),
                          (masked, SEED_HEAD), (pt_ready, SEED_HEAD), (pv_done, SEED_PAIR), (recip_done, SEED_PAIR),
                          (mixed_done, SEED_PAIR), (rot_done, SEED_ROT), (rot_read, SEED_ROT_READ), (qk_done, SEED_QK),
                          (conv_done, SEED_CONV), (prod_done, SEED_PROD), (act_lo_done, SEED_PROD), (branch_sq, SEED_SQ)):
                dve.sem_inc(s_, n)
            dve.wait_ge(par_landed, 16)
            for i in range(XPARTS):
                dve.wait_ge(x_landed[i], 16)
                for c in range(i * KC // XPARTS, (i + 1) * KC // XPARTS):
                    h_chunk_lo(0, c, h_hi, h_lo, par[:, O_LN1 + c:O_LN1 + c + 1])
                if i < RING:
                    lo(0, i)
            dve.wait_ge(id_landed, 16)
            with dve.Fori(0, DEPTH) as l:
                lg = l * GROUPS
                for s in range(RING):
                    lo(lg + 1, s)
                lo(lg + 2, 0)
                lo(lg + 2, 1)
                norm_mean(2 * l)
                lo(lg + 2, 2)
                norm_diag(2 * l)
                lo(lg + 2, 3)
                norm_end(2 * l)
                with dve.Fori(2, 2 * NVB) as i:
                    for s in range(RING):
                        lo(lg + i + 1, s)

                dve.wait_ge(r_all_done, 2 * l + 1)
                dve.wait_ge(con_landed, 16)
                dve.wait_ge(mask_landed, 16)
                masks_a, masks_b = (mask_a, mask_a), (mask_b, mask_b)

                def step_a(i, pairs_before):
                    g = lg + i + (G_PROJ + 1)
                    lo(g, 0)
                    if pairs_before >= 2:
                        recip(l, i - 2)
                    if pairs_before >= 1:
                        rotated(l, i - 1, 1, i - 1, False)
                    take_raw(l, i, 0, True)
                    lo(g, 1)
                    lo(g, 2)
                    take_raw(l, i, 1, False)
                    lo(g, 3)
                    if pairs_before >= 2:
                        outputs(l, i - 2)
                    if pairs_before >= 1:
                        mask(l, i - 1, masks_a)
                    rotated(l, i, 0, i, True)

                step_a(0, 0)
                step_a(1, 1)
                with dve.Fori(2, PA) as i:
                    step_a(i, 2)
                g = lg + (G_PROJ + PA + 1)
                lo(g, 0)
                recip(l, PA - 2)
                rotated(l, PA - 1, 1, PA - 1, False)
                take_raw(l, PA, 0, False)
                lo(g, 1)
                lo(g, 2)
                take_raw(l, PA, 1, True)
                lo(g, 3)
                outputs(l, PA - 2)
                mask(l, PA - 1, masks_a)
                rotated(l, PA, 0, PA, False)
                rotated(l, PA, 1, PA, True)
                for j in range(1, PB):
                    r = 2 * PA + 1 + j
                    g = lg + (G_PROJ + r // 2 + 1)
                    lo(g, 2 * (r % 2))
                    take_raw(l, r // 2, r % 2, True)
                    lo(g, 2 * (r % 2) + 1)
                    recip(l, PA + j - 2, sink=j - 2 if j >= 2 else None)
                    mask(l, PA + j - 1, masks_b, sink=j - 1)
                    rotated(l, r // 2, r % 2, PA + j, True)
                    outputs(l, PA + j - 2)
                for i in range(PC):
                    g = lg + (G_PROJ + PA + 3 + i + 1)
                    pair = PA + PB + i
                    if i == 1:
                        dve.wait_ge(bias_ready, HC * (l + 1))
                    recip(l, pair - 2, sink=PB - 2 + i if i < 2 else None)
                    lo(g, 0)
                    if i == 0:
                        mask(l, pair - 1, masks_b, sink=PB - 1)
                    else:
                        mask(l, pair - 1, (bias[:, 2 * i - 2], bias[:, 2 * i - 1]))
                    take_c(l, i, 0)
                    lo(g, 1)
                    lo(g, 2)
                    if i in (2, 4):
                        branch_mean(l, i // 2 - 1)
                    take_c(l, i, 1)
                    lo(g, 3)
                    outputs(l, pair - 2)
                    if i in (2, 4):
                        branch_scale(l, i // 2 - 1)
                recip(l, PAIRS - 2)
                mask(l, PAIRS - 1, (bias[:, HC - 2], bias[:, HC - 1]))
                outputs(l, PAIRS - 2)
                for c in range(3):
                    mix_lo(l, c)
                recip(l, PAIRS - 1)
                mix_lo(l, 3)
                mix_lo(l, 4)
                outputs(l, PAIRS - 1)
                branch_mean(l, 2)
                mix_lo(l, 5)
                branch_scale(l, 2)
                for c in range(6, KC):
                    mix_lo(l, c)
                    if c == 12:
                        lo(lg + (G_OUT + 1), 0)

                def out_chunks(i, first):
                    g = lg + i + G_OUT
                    for b in range(2):
                        if not (first and b == 0):
                            lo(g + 1, 2 * b)
                        add_to_x(g, 1 + 2 * b, 2 * i + b, b, l * (2 * KC) + 2 * i + (b + 1))
                        lo(g + 1, 2 * b + 1)
                        h_chunk_lo(2 * l + 1, 2 * i + b, h2_hi, h2_lo,
                                   par[:, bass.ds(l * NPAR + 2 * i + (O_LN2 + b), 1)])

                out_chunks(0, True)
                with dve.Fori(1, KC // 2) as i:
                    out_chunks(i, False)

                def quarter(q, first, last):
                    g0 = lg + q * G_QUARTER

                    def up(j, cols):
                        g = g0 + j + (G_FFN + 1)
                        f = q * FQ + j
                        col = l * NPAR + 8 * f
                        for b, u in ((0, gate), (1, value)):
                            lo(g, 2 * b, cols)
                            dve.wait_ge(r_all_done, 2 * l + 2)
                            dve.wait_ge(slot_used, RING * (g - 1) + (1 + 2 * b + SEED_SLOT + 1))
                            dve.wait_ge(conv_done, l * (2 * FC) + 2 * f + (b - 1 + SEED_CONV))
                            dve.tensor_tensor(z[:, b], acc[b][:, 0:T], r_all[:], ALU.mult).then_inc(acc_free[b], 1)
                            if b == 0 or cols == PIECE:
                                lo(g, 2 * b + 1, cols)
                            dve.wait_ge(affine_done, l * (2 * FC) + 2 * f + (b + 1))
                            dve.scalar_tensor_tensor(u[:, 1:T], z[:, b, 0:T - 1],
                                                     par[:, bass.ds(col + (O_CONV + 4 * b), 1)], u[:, 1:T],
                                                     ALU.mult, ALU.add).then_inc(tap_done, 1)
                            dve.wait_ge(tap_done, l * (2 * FC) + 2 * f + (b + 1))
                            dve.scalar_tensor_tensor(u[:, 0:T - 1], z[:, b, 1:T],
                                                     par[:, bass.ds(col + (O_CONV + 4 * b + 2), 1)], u[:, 0:T - 1],
                                                     ALU.mult, ALU.add).then_inc(conv_done, 1)
                        if cols != PIECE:
                            lo(g, 3, cols)

                    if first:
                        norm_mean(2 * l + 1)
                        norm_diag(2 * l + 1)
                        norm_end(2 * l + 1)
                    with dve.Fori(0, FQ - 1) as j:
                        up(j, PIECE)
                    up(FQ - 1, PIECE_DOWN)

                    def down_add(i, s):
                        add_to_x(g0 + i + (G_FFN + G_UP), s, 4 * i + s, s % 2, l * (2 * KC) + 4 * i + (KC + s + 1))

                    def down_lo(i, s):
                        if last:
                            h_chunk_lo(2 * l + 2, 4 * i + s, h_hi, h_lo,
                                       par[:, bass.ds(l * NPAR + 4 * i + (NPAR + O_LN1 + s), 1)])

                    with dve.Fori(0, G_DOWN - 1) as i:
                        for s in range(RING):
                            down_add(i, s)
                            lo(g0 + i + (G_FFN + G_UP + 1), s, PIECE_DOWN)
                            down_lo(i, s)
                    for s in range(RING):
                        down_add(G_DOWN - 1, s)
                        down_lo(G_DOWN - 1, s)
                        if not last:
                            lo(g0 + (G_FFN + G_QUARTER), s)
                        else:
                            with dve.If(l < DEPTH - 1):
                                lo(g0 + (G_FFN + G_QUARTER), s)

                quarter(0, True, False)
                with dve.Fori(1, QUARTERS - 1) as q:
                    quarter(q, False, False)
                quarter(QUARTERS - 1, False, True)
            norm_mean(2 * DEPTH)
            norm_diag(2 * DEPTH)
            norm_end(2 * DEPTH)
            dve.wait_ge(r_all_done, 2 * DEPTH + 1)
            for c in range(Y_POOL):
                dve.scalar_tensor_tensor(as_chunks[:, c], x[:, c], par[:, DEPTH * NPAR + c:DEPTH * NPAR + c + 1], r_all[:],
                                         ALU.mult, ALU.mult).then_inc(y_done, 1)

        @block.gpsimd
        def _(pool):
            pool.memset(minus_half[:], -0.5).then_inc(half_set, 1)
            pool.memset(zeros[:], 0.0).then_inc(zeros_set, 1)
            pool.wait_ge(zeros_set, 1)

            def squares_begin():
                pool.tensor_tensor(sq_sum[:], zeros[:], zeros[:], ALU.add).then_inc(sum_done, 1)

            def square(n, c, count=1):
                xc = x[:, bass.ds(c, 1)].rearrange("p a t -> p (a t)")
                pool.wait_ge(sum_done, n * (KC + 1) + c + 1)
                pool.tensor_tensor(sq[:], xc, xc, ALU.mult).then_inc(sq_done, count)
                pool.wait_ge(sq_done, n * KC + c + 1)
                pool.tensor_tensor(sq_sum[:], sq_sum[:], sq[:], ALU.add).then_inc(sum_done, 1)

            def norm(n):
                pool.wait_ge(ms_done, n + 1)
                pool.tensor_tensor(r_tok[:], ms[:], minus_half[:], ALU.pow).then_inc(r_tok_done, 1)

            def cos_product(l, i, b):
                pool.wait_ge(raw_hi_done, l * ROT + 2 * i + (b + 1))
                pool.tensor_tensor(raw_lo[:, b], raw[b][:], raw_hi[:, b].bitcast(F32),
                                   ALU.subtract).then_inc(raw_lo_done, 1)
                pool.wait_ge(rot_done, l * ROT + 2 * i + (b + SEED_ROT))
                pool.tensor_tensor(rot_cos[:], raw[b][:], cos, ALU.mult).then_inc(cos_done, 1)

            def branch_rsqrt(l, br):
                pool.wait_ge(branch_ms_done, 3 * l + (br + 1))
                pool.tensor_tensor(branch_r[:, br], branch_ms[:, br], minus_half[:], ALU.pow).then_inc(branch_r_done, 1)

            squares_begin()
            for c in range(SQ_POOL):
                pool.wait_ge(x_landed[c * XPARTS // KC], 16)
                square(0, c, 1 if c < SQ_POOL - 1 else 1 + KC - SQ_POOL)
            for c in range(SQ_POOL, KC):
                pool.wait_ge(first_squares, c - SQ_POOL + 1)
                pool.wait_ge(sum_done, c + 1)
                pool.tensor_tensor(sq_sum[:], sq_sum[:], as_chunks[:, c], ALU.add).then_inc(sum_done, 1)
            pool.wait_ge(half_set, 1)
            pool.dma_start(con[:, 0:O_ID], consts[:, 0:O_ID]).then_inc(con_landed, 16)
            pool.dma_start(con[:, O_MASK:NCONST], consts[:, O_MASK:NCONST]).then_inc(mask_landed, 16)
            pool.wait_ge(con_landed, 16)
            pool.tensor_tensor(rot_r[:], rot_m, zeros[:, 0:P], ALU.add).then_inc(rot_r_set, 1)
            with pool.Fori(0, DEPTH) as l:
                pool.dma_start(bias[:], bias_c[bass.ds(l, 1)].rearrange("a p h c -> (a p) h c")).then_inc(bias_landed, 16)
                norm(2 * l)
                pool.wait_ge(con_landed, 16)
                pool.wait_ge(mask_landed, 16)
                pool.wait_ge(bias_landed, 16 * l + 16)
                for hc in range(HC):
                    pool.tensor_tensor(bias[:, hc], bias[:, hc], mask_c, ALU.add).then_inc(bias_ready, 1)
                with pool.Fori(0, ROT // 2) as i:
                    cos_product(l, i, 0)
                    cos_product(l, i, 1)
                for br in range(3):
                    branch_rsqrt(l, br)
                pool.wait_ge(ssq_ready, 2 * l + 1)
                squares_begin()
                with pool.Fori(0, KC // 2) as i:
                    for b in range(2):
                        pool.wait_ge(acc_free[b], l * ROUNDS + i + (R_OUT + SEED_ACC + 1))
                        square(2 * l + 1, 2 * i + b)
                norm(2 * l + 1)
                with pool.Fori(0, QUARTERS) as q:
                    with pool.Fori(0, FQ) as j:
                        f = q * FQ + j
                        pool.wait_ge(silu_done, l * FC + f + 1)
                        pool.wait_ge(conv_done, l * (2 * FC) + 2 * f + (2 + SEED_CONV))
                        pool.wait_ge(act_lo_done, l * FC + f + SEED_PROD)
                        pool.tensor_tensor(prod[:], silu[:], value[:], ALU.mult).then_inc(prod_done, 1)
                        pool.wait_ge(act_hi_done, l * FC + f + 1)
                        at = bass.ds(j, 1)
                        pool.tensor_tensor(act_lo[:, at].rearrange("p a t -> p (a t)"), prod[:],
                                           act_hi[:, at].rearrange("p a t -> p (a t)").bitcast(F32),
                                           ALU.subtract).then_inc(act_lo_done, 1)
                pool.wait_ge(sum_done, (2 * l + 2) * (KC + 1))
                pool.wait_ge(ssq_ready, 2 * l + 2)
                squares_begin()
                with pool.Fori(0, KC // 2) as i:
                    for b in range(2):
                        pool.wait_ge(acc_free[b], l * ROUNDS + i
                                     + (QUARTERS * R_QUARTER - R_QUARTER + R_FFN + FQ + SEED_ACC + 1))
                        square(2 * l + 2, 2 * i + b)
            norm(2 * DEPTH)
            pool.wait_ge(r_all_done, 2 * DEPTH + 1)
            for c in range(Y_POOL, KC):
                pool.wait_ge(scaled_done, c - Y_POOL + 1)
                pool.tensor_tensor(as_chunks[:, c], as_chunks[:, c], r_all[:], ALU.mult).then_inc(y_pool_done, 1)


def _constants():
    f32 = np.float32
    inv = (f32(10000.0) ** (-np.arange(0, HD, 2, dtype=f32) / f32(HD))).astype(f32)
    ang = np.arange(T, dtype=f32)[:, None] * inv[None, :]
    four = np.tile(ang.T, (4, 1))
    swap = np.zeros((P, P), f32)
    half = HD // 2
    for base in (0, HD):
        for d in range(half):
            swap[base + half + d, base + d] = -1.0
            swap[base + d, base + half + d] = 1.0
    q, k = np.arange(T)[:, None], np.arange(T)[None, :]
    times = np.zeros((T, T))
    for window, r in ((128, 1), (512, 4), (2048, 16)):
        times += (q % r == k % r) & (np.abs(q // r - k // r) <= window // (2 * r))
    m_a = np.where(times > 0, np.log(np.maximum(times, 1.0)), NEG)
    m_b = np.where(np.abs(q - k) <= 128, 0.0, NEG)
    start = np.clip(q % 64 - 8, 0, 64 - 16)
    m_c = np.where((k % 64 >= start) & (k % 64 < start + 16), 0.0, NEG)
    tiled = [m.reshape(TT, P, T).transpose(1, 0, 2).reshape(P, TT * T).astype(f32) for m in (m_a, m_b, m_c)]
    return np.ascontiguousarray(np.concatenate(
        [np.cos(four), np.sin(four), swap, np.eye(P, dtype=f32), np.ones((P, P), f32), *tiled], 1).astype(f32))


def _chunks(w):
    n = w.shape[1] // P
    return w.reshape(2, 8, P, n, P).transpose(3, 0, 2, 1, 4).reshape(n, 2, P, PIECE)


def kernel(**inputs):
    import concourse.bacc as bacc
    from concourse.bass_utils import run_bass_kernel_spmd

    a = {k: np.asarray(v_) for k, v_ in inputs.items()}
    heads_b = [j + h * PB for j in range(PB) for h in range(HKV)]
    w_main, w_up, w_down, params, biases = [], [], [], [], []
    at = np.cumsum([0, WA, WA, WA, WB, WKV, WKV, WC, WC, WC])
    row = np.arange(T)
    cols_off = np.clip(row[None, :] % 64 - row[:, None] % 64 + 15, 0, 30)
    rows_off = row[None, :] // 64 - row[:, None] // 64 + 7
    for l in range(DEPTH):
        qa, ka, va, qb, kb, vb, qc, kc, vc = (a["w_in"][l][:, at[i]:at[i + 1]] for i in range(9))
        qb = qb.reshape(D, HB, HD)[:, heads_b].reshape(D, WB)
        wv = np.concatenate([va, vb, vc], 1)
        v_pieces = wv.reshape(8, 2, P, NVB, 512).transpose(3, 0, 2, 1, 4).reshape(-1, P, PIECE)

        def by_turns(wq, wk):
            return np.stack([_chunks(wq), _chunks(wk)], 1).reshape(-1, P, PIECE)

        order = [slice(0, WA), None, slice(WA + WB, D)]
        wo = a["w_out"][l]
        wo_b = wo[WA:WA + WB].reshape(HB, HD, D)[heads_b].reshape(WB, D)
        wo = np.concatenate([wo[order[0]], wo_b, wo[order[2]]], 0)
        mg = a["mix_gain"][l]
        mg = np.concatenate([mg[:WA], mg[WA:WA + WB].reshape(HB, HD)[heads_b].reshape(-1), mg[WA + WB:]])
        w_main.append(np.concatenate([
            v_pieces, by_turns(qa, ka), _chunks(np.concatenate([kb, qb], 1)).reshape(-1, P, PIECE),
            by_turns(qc, kc), _chunks(wo).reshape(-1, P, PIECE)]).reshape(MAIN, RING, P, PIECE))
        up = a["w_up"][l]
        w_up.append(by_turns(up[:, :D_FF], up[:, D_FF:]).reshape(FC, RING, P, PIECE))
        w_down.append(a["w_down"][l].reshape(QUARTERS, FQ, P, KC, P).transpose(0, 3, 2, 1, 4)
                      .reshape(QUARTERS * G_DOWN, RING, P, PIECE_DOWN))
        conv = np.concatenate([a["conv_w"][l], a["conv_b"][l][None]], 0).reshape(4, 2, FC, P)
        params += [a["ln_attn"][l].reshape(KC, P).T, mg.reshape(KC, P).T, a["ln_ffn"][l].reshape(KC, P).T,
                   conv.transpose(3, 2, 1, 0).reshape(P, 8 * FC),
                   np.broadcast_to(a["sink_b"][l][heads_b], (P, HB))]
        rpb = a["rpb_c"][l][:, rows_off, cols_off]
        biases.append(rpb.reshape(HC, TT, P, T).transpose(2, 0, 1, 3).reshape(P, HC, TT * T))
    params.append(a["ln_final"].reshape(KC, P).T)
    arrays = {
        "in_x": a["x"][0].reshape(T, KC, P).transpose(2, 1, 0),
        "in_w_main": np.stack(w_main).reshape(DEPTH * MAIN, RING, P, PIECE),
        "in_w_up": np.stack(w_up).reshape(DEPTH * FC, RING, P, PIECE),
        "in_w_down": np.stack(w_down).reshape(DEPTH * QUARTERS * G_DOWN, RING, P, PIECE_DOWN),
        "in_bias_c": np.stack(biases),
        "in_params": np.concatenate(params, 1),
        "in_consts": _constants(),
    }
    arrays = {k: np.ascontiguousarray(v_) for k, v_ in arrays.items()}
    nc = bacc.Bacc("TRN2", target_bir_lowering=False, num_devices=1)
    args = [nc.dram_tensor(n, v_.shape, F32, kind="ExternalInput").ap() for n, v_ in arrays.items()]
    args.append(nc.dram_tensor("out_y", (P, KC, T), F32, kind="ExternalOutput").ap())
    build(nc, *args)
    r = run_bass_kernel_spmd(nc, [arrays], core_ids=[0])
    y = np.asarray(r.results[0]["out_y"])
    return y.transpose(2, 1, 0).reshape(1, T, D)
```
